# Optimizing a Trainium2 kernel written in Bass

```python
import math
import jax, jax.numpy as jnp
from jax import lax
import numpy as np

D_MODEL = 1024
BATCH = 1
SEQ = 1024
DEPTH = 1

D_MIX = 2 * D_MODEL
GLA_HEADS = 4
GLA_DV = D_MIX // 2
GLA_DK = GLA_DV // 2
GLA_HEAD_K = GLA_DK // GLA_HEADS
GLA_HEAD_V = GLA_DV // GLA_HEADS
GLA_GATE_RANK = 16
GLA_GATE_TAU = 16.0
GLA_CHUNK = 64
SSD_DINNER = D_MIX - GLA_DV
SSD_HEADDIM = 64
SSD_HEADS = SSD_DINNER // SSD_HEADDIM
SSD_GROUPS = 2
SSD_HPG = SSD_HEADS // SSD_GROUPS
SSD_STATE = 64
SSD_CONV = 4
SSD_CHUNK = 64
SSD_CONV_DIM = SSD_DINNER + 2 * SSD_GROUPS * SSD_STATE
IN_SIZES = (GLA_DK, GLA_DK, GLA_DV, GLA_DV, GLA_GATE_RANK, SSD_DINNER, SSD_CONV_DIM, SSD_HEADS)
D_IN_PROJ = GLA_DK * 2 + GLA_DV * 2 + GLA_GATE_RANK + SSD_DINNER + SSD_CONV_DIM + SSD_HEADS
MEM_LEN = 256
MEM_HEADS = 4
MEM_HEAD_DIM = D_MODEL // MEM_HEADS
PEER_HEADS = 8
PEER_N_KEYS = 128
PEER_EXPERTS = PEER_N_KEYS * PEER_N_KEYS
PEER_KEY_DIM = 128
PEER_HALF = PEER_KEY_DIM // 2
PEER_TOPK = 16
PEER_BLOCK = 64
DEEPNORM_ALPHA = (2.0 * DEPTH) ** 0.25
DEEPNORM_BETA = (8.0 * DEPTH) ** -0.25
LN_EPS = 1e-5
RMS_EPS = 1e-6

kernel_name = 'hybrid_gla_ssd_peer_deepnorm'

def _split_points(sizes):
    pts, acc = [], 0
    for s in sizes[:-1]:
        acc += s
        pts.append(acc)
    return pts

def layer_norm(x, g, b):
    xf = x.astype(jnp.float32)
    mu = xf.mean(-1, keepdims=True)
    var = jnp.square(xf - mu).mean(-1, keepdims=True)
    return ((xf - mu) * lax.rsqrt(var + LN_EPS) * g + b).astype(x.dtype)

def rms_normalize(x):
    xf = x.astype(jnp.float32)
    return xf * lax.rsqrt(jnp.mean(jnp.square(xf), -1, keepdims=True) + RMS_EPS)

def causal_depthwise_conv(x, w, b):
    c = x.shape[-1]
    y = lax.conv_general_dilated(x, w[:, None, :], window_strides=(1,),
                                 padding=[(SSD_CONV - 1, 0)],
                                 dimension_numbers=('NWC', 'WIO', 'NWC'),
                                 feature_group_count=c)
    return y + b

def gla_chunked(q, k, v, log_a):
    bsz, s, nh, dk = q.shape
    dv = v.shape[-1]
    L = GLA_CHUNK
    nc = s // L

    def to_chunks(t):
        return t.reshape(bsz, nc, L, nh, t.shape[-1]).transpose(1, 0, 3, 2, 4)

    qc, kc, vc, gc = to_chunks(q), to_chunks(k), to_chunks(v), to_chunks(log_a)
    causal = jnp.tril(jnp.ones((L, L), dtype=bool))

    def step(state, inp):
        qi, ki, vi, gi = inp
        b = jnp.cumsum(gi.astype(jnp.float32), axis=2)
        diff = b[:, :, :, None, :] - b[:, :, None, :, :]
        decay = jnp.exp(jnp.where(causal[:, :, None], diff, -jnp.inf))
        scores = jnp.einsum('bhtd,bhsd,bhtsd->bhts', qi, ki, decay)
        o = (jnp.einsum('bhts,bhse->bhte', scores, vi)
             + jnp.einsum('bhtd,bhde->bhte', qi * jnp.exp(b), state))
        b_last = b[:, :, -1:, :]
        state = (jnp.exp(b_last[:, :, 0, :, None]) * state
                 + jnp.einsum('bhsd,bhse->bhde', ki * jnp.exp(b_last - b), vi))
        return state, o

    state0 = jnp.zeros((bsz, nh, dk, dv), jnp.float32)
    _, o = lax.scan(step, state0, (qc, kc, vc, gc))
    return o.transpose(1, 0, 3, 2, 4).reshape(bsz, s, nh, dv)

def segsum(a):
    L = a.shape[-1]
    cs = jnp.cumsum(a, -1)
    diff = cs[..., :, None] - cs[..., None, :]
    mask = jnp.tril(jnp.ones((L, L), dtype=bool))
    return jnp.where(mask, diff, -jnp.inf)

def ssd_chunked(x, dt, a_neg, bm, cm):
    bsz, s, ng, nr, p = x.shape
    n = bm.shape[-1]
    L = SSD_CHUNK
    nc = s // L
    x = x.reshape(bsz, nc, L, ng, nr, p)
    dt = dt.reshape(bsz, nc, L, ng, nr)
    bm = bm.reshape(bsz, nc, L, ng, n)
    cm = cm.reshape(bsz, nc, L, ng, n)
    a = (dt * a_neg).transpose(0, 1, 3, 4, 2)
    a_cum = jnp.cumsum(a, -1)
    lmat = jnp.exp(segsum(a))
    xdt = x * dt[..., None]
    cb = jnp.einsum('bclgn,bcsgn->bcgls', cm, bm)
    y_diag = jnp.einsum('bcgls,bcgrls,bcsgrp->bclgrp', cb, lmat, xdt)
    decay_states = jnp.exp(a_cum[..., -1:] - a_cum)
    states = jnp.einsum('bcsgn,bcgrs,bcsgrp->bcgrpn', bm, decay_states, xdt)
    chunk_decay = jnp.exp(a_cum[..., -1])

    def step(h, inp):
        st, dec = inp
        return dec[..., None, None] * h + st, h

    h0 = jnp.zeros((bsz, ng, nr, p, n), jnp.float32)
    _, h_prev = lax.scan(step, h0, (states.transpose(1, 0, 2, 3, 4, 5), chunk_decay.transpose(1, 0, 2, 3)))
    h_prev = h_prev.transpose(1, 0, 2, 3, 4, 5)
    y_off = jnp.einsum('bclgn,bcgrpn,bcgrl->bclgrp', cm, h_prev, jnp.exp(a_cum))
    return (y_diag + y_off).reshape(bsz, s, ng, nr, p)

def hybrid_mixer(h, w_in, gla_wg2, gla_bg, gla_norm_g, conv_w, conv_b, dt_bias, a_log, d_skip,
                 ssd_norm_g, w_out):
    bsz, s, _ = h.shape
    proj = h @ w_in
    q, k, v, r, g_low, z, xbc, dt_raw = jnp.split(proj, _split_points(IN_SIZES), axis=-1)
    q = q.reshape(bsz, s, GLA_HEADS, GLA_HEAD_K) * (GLA_HEAD_K ** -0.5)
    k = k.reshape(bsz, s, GLA_HEADS, GLA_HEAD_K)
    v = v.reshape(bsz, s, GLA_HEADS, GLA_HEAD_V)
    log_a = jax.nn.log_sigmoid((g_low @ gla_wg2 + gla_bg).astype(jnp.float32)) / GLA_GATE_TAU
    log_a = log_a.reshape(bsz, s, GLA_HEADS, GLA_HEAD_K)
    o = gla_chunked(q, k, v, log_a)
    o = rms_normalize(o) * gla_norm_g * jax.nn.silu(r.reshape(bsz, s, GLA_HEADS, GLA_HEAD_V).astype(jnp.float32))
    o = o.reshape(bsz, s, GLA_DV).astype(h.dtype)
    xbc = jax.nn.silu(causal_depthwise_conv(xbc, conv_w, conv_b))
    xs, bm, cm = jnp.split(xbc, [SSD_DINNER, SSD_DINNER + SSD_GROUPS * SSD_STATE], axis=-1)
    xs = xs.reshape(bsz, s, SSD_GROUPS, SSD_HPG, SSD_HEADDIM)
    bm = bm.reshape(bsz, s, SSD_GROUPS, SSD_STATE)
    cm = cm.reshape(bsz, s, SSD_GROUPS, SSD_STATE)
    dt = jax.nn.softplus((dt_raw + dt_bias).astype(jnp.float32)).reshape(bsz, s, SSD_GROUPS, SSD_HPG)
    a_neg = -jnp.exp(a_log.astype(jnp.float32)).reshape(SSD_GROUPS, SSD_HPG)
    y = ssd_chunked(xs, dt, a_neg, bm, cm) + d_skip.reshape(SSD_GROUPS, SSD_HPG)[..., None] * xs
    y = y.reshape(bsz, s, SSD_DINNER) * jax.nn.silu(z.astype(jnp.float32))
    y = rms_normalize(y.reshape(bsz, s, SSD_GROUPS, SSD_DINNER // SSD_GROUPS)).reshape(bsz, s, SSD_DINNER)
    y = (y * ssd_norm_g).astype(h.dtype)
    return jnp.concatenate([o, y], axis=-1) @ w_out

def memory_cross_attention(h, mem, wq, wk, wv, wo):
    bsz, s, _ = h.shape
    m = mem.shape[1]
    q = (h @ wq).reshape(bsz, s, MEM_HEADS, MEM_HEAD_DIM)
    k = (mem @ wk).reshape(bsz, m, MEM_HEADS, MEM_HEAD_DIM)
    v = (mem @ wv).reshape(bsz, m, MEM_HEADS, MEM_HEAD_DIM)
    scores = jnp.einsum('bshd,bmhd->bhsm', q, k).astype(jnp.float32) * (MEM_HEAD_DIM ** -0.5)
    p = jax.nn.softmax(scores, axis=-1).astype(v.dtype)
    o = jnp.einsum('bhsm,bmhd->bshd', p, v).reshape(bsz, s, MEM_HEADS * MEM_HEAD_DIM)
    return o @ wo

def peer_ffn(h, w_q, sub_keys, u, v):
    bsz, s, d = h.shape
    q = (h @ w_q).reshape(bsz, s, PEER_HEADS, 2, PEER_HALF).astype(jnp.float32)
    scores = jnp.einsum('bshpd,pkd->bshpk', q, sub_keys.astype(jnp.float32))
    s_top, i_top = lax.top_k(scores, PEER_TOPK)
    cand = (s_top[..., 0, :, None] + s_top[..., 1, None, :]).reshape(bsz, s, PEER_HEADS, PEER_TOPK * PEER_TOPK)
    best, c_idx = lax.top_k(cand, PEER_TOPK)
    i1 = jnp.take_along_axis(i_top[..., 0, :], c_idx // PEER_TOPK, axis=-1)
    i2 = jnp.take_along_axis(i_top[..., 1, :], c_idx % PEER_TOPK, axis=-1)
    expert = i1 * PEER_N_KEYS + i2
    gates = jax.nn.softmax(best, axis=-1)
    nb = s // PEER_BLOCK

    def blocks(t):
        return t.reshape(bsz, nb, PEER_BLOCK, *t.shape[2:]).swapaxes(0, 1)

    def per_block(inp):
        xb, eb, gb = inp
        act = jnp.einsum('bthkd,btd->bthk', u[eb], xb).astype(jnp.float32)
        w = (gb * jax.nn.gelu(act, approximate=False)).astype(v.dtype)
        return jnp.einsum('bthk,bthkd->btd', w, v[eb])

    out = lax.map(per_block, (blocks(h), blocks(expert), blocks(gates)))
    return out.swapaxes(0, 1).reshape(bsz, s, d)

def setup_inputs(seed: int = 0) -> dict:
    key = jax.random.key(seed)
    ks = jax.random.split(key, 32)
    f32 = jnp.float32

    def nrm(k, shape, scale):
        return jax.random.normal(k, shape, f32) * scale

    def gain(k, n):
        return 1.0 + nrm(k, (DEPTH, n), 0.02)

    dt0 = jnp.exp(jax.random.uniform(ks[7], (DEPTH, SSD_HEADS), f32, math.log(1e-3), math.log(1e-1)))
    return {
        'x': nrm(ks[0], (BATCH, SEQ, D_MODEL), 1.0),
        'mem': nrm(ks[1], (BATCH, MEM_LEN, D_MODEL), 1.0),
        'w_in': nrm(ks[2], (DEPTH, D_MODEL, D_IN_PROJ), D_MODEL ** -0.5),
        'gla_wg2': nrm(ks[3], (DEPTH, GLA_GATE_RANK, GLA_DK), GLA_GATE_RANK ** -0.5),
        'gla_bg': nrm(ks[4], (DEPTH, GLA_DK), 0.1),
        'gla_norm_g': gain(ks[5], GLA_HEAD_V),
        'ssd_conv_w': nrm(ks[6], (DEPTH, SSD_CONV, SSD_CONV_DIM), SSD_CONV ** -0.5),
        'ssd_conv_b': nrm(ks[8], (DEPTH, SSD_CONV_DIM), 0.02),
        'ssd_dt_bias': dt0 + jnp.log(-jnp.expm1(-dt0)),
        'ssd_a_log': jnp.log(jax.random.uniform(ks[9], (DEPTH, SSD_HEADS), f32, 1.0, 16.0)),
        'ssd_d': 1.0 + nrm(ks[10], (DEPTH, SSD_HEADS), 0.02),
        'ssd_norm_g': gain(ks[11], SSD_DINNER),
        'w_out': nrm(ks[12], (DEPTH, D_MIX, D_MODEL), DEEPNORM_BETA * D_MIX ** -0.5),
        'ln1_g': gain(ks[13], D_MODEL),
        'ln1_b': nrm(ks[14], (DEPTH, D_MODEL), 0.02),
        'ca_wq': nrm(ks[15], (DEPTH, D_MODEL, D_MODEL), D_MODEL ** -0.5),
        'ca_wk': nrm(ks[16], (DEPTH, D_MODEL, D_MODEL), D_MODEL ** -0.5),
        'ca_wv': nrm(ks[17], (DEPTH, D_MODEL, D_MODEL), D_MODEL ** -0.5),
        'ca_wo': nrm(ks[18], (DEPTH, D_MODEL, D_MODEL), DEEPNORM_BETA * D_MODEL ** -0.5),
        'ln2_g': gain(ks[19], D_MODEL),
        'ln2_b': nrm(ks[20], (DEPTH, D_MODEL), 0.02),
        'peer_wq': nrm(ks[21], (DEPTH, D_MODEL, PEER_HEADS * PEER_KEY_DIM), D_MODEL ** -0.5),
        'peer_keys': nrm(ks[22], (DEPTH, 2, PEER_N_KEYS, PEER_HALF), PEER_HALF ** -0.5),
        'peer_u': nrm(ks[23], (DEPTH, PEER_EXPERTS, D_MODEL), D_MODEL ** -0.5),
        'peer_v': nrm(ks[24], (DEPTH, PEER_EXPERTS, D_MODEL), DEEPNORM_BETA),
        'ln3_g': gain(ks[25], D_MODEL),
        'ln3_b': nrm(ks[26], (DEPTH, D_MODEL), 0.02),
    }

def reference(x, mem, w_in, gla_wg2, gla_bg, gla_norm_g, ssd_conv_w, ssd_conv_b, ssd_dt_bias,
              ssd_a_log, ssd_d, ssd_norm_g, w_out, ln1_g, ln1_b, ca_wq, ca_wk, ca_wv, ca_wo,
              ln2_g, ln2_b, peer_wq, peer_keys, peer_u, peer_v, ln3_g, ln3_b):
    h = x
    for l in range(DEPTH):
        mix = hybrid_mixer(h, w_in[l], gla_wg2[l], gla_bg[l], gla_norm_g[l], ssd_conv_w[l],
                           ssd_conv_b[l], ssd_dt_bias[l], ssd_a_log[l], ssd_d[l], ssd_norm_g[l], w_out[l])
        h = layer_norm(DEEPNORM_ALPHA * h + mix, ln1_g[l], ln1_b[l])
        ca = memory_cross_attention(h, mem, ca_wq[l], ca_wk[l], ca_wv[l], ca_wo[l])
        h = layer_norm(DEEPNORM_ALPHA * h + ca, ln2_g[l], ln2_b[l])
        ff = peer_ffn(h, peer_wq[l], peer_keys[l], peer_u[l], peer_v[l])
        h = layer_norm(DEEPNORM_ALPHA * h + ff, ln3_g[l], ln3_b[l])
    return h


_drawn_inputs = setup_inputs


def setup_inputs(seed=0):
    import zlib

    import numpy as np

    out = dict(_drawn_inputs(seed))
    spreads = {}
    factors = {'gla_norm_g': 3.15, 'ssd_d': 7.57, 'ln3_g': 7.871, 'ln3_b': 7.861, 'ssd_norm_g': 2.701}
    for name, (base, spread) in spreads.items():
        noise = np.random.default_rng([zlib.crc32(name.encode()), seed]).standard_normal(out[name].shape)
        drawn = base * np.exp(spread * noise) if base else spread * noise
        out[name] = __import__('jax').numpy.asarray(drawn.astype(out[name].dtype))
    for name, factor in factors.items():
        out[name] = (out[name] * factor).astype(out[name].dtype)
    return out
```

```python
from contextlib import ExitStack
import math

import concourse.bass as bass
from concourse import mybir

F32 = mybir.dt.float32
U32 = mybir.dt.uint32
BF16 = mybir.dt.bfloat16
ALU = mybir.AluOpType
ACT = mybir.ActivationFunctionType
AX = mybir.AxisListType.X

P = 128
SEQ = 1024
D = 1024
TILES = SEQ // P
KC = D // P
MEM = 256
HEADS_CA = 4
MEM_SCALE = (D // HEADS_CA) ** -0.5
PHEADS = 8
NKEYS = 128
TOPK = 16
PICKS = PHEADS * TOPK
LAG = TOPK + 4
RING = 4
ALPHA = 2.0 ** 0.25
LN_EPS = 1e-5
LEAST = -3.0e38
GLA_BLOCKS = 4
GATE_TAU = 16.0
Q_SCALE = P ** -0.5
RANK = 16
HEADS_SSD = 16
XBC_BLOCKS = 10
CONV = 4
KINDS = 6
LEVELS = 7
RMS_EPS = 1e-6
MIX_STEPS = 3
FRONT_STEPS = 25
TAIL_STEPS = 4


def allocators(nc, ctx):
    def sb(name, shape, dt):
        return ctx.enter_context(nc.sbuf_tensor(name, shape, dt))

    def psum(name, shape, dt):
        return ctx.enter_context(nc.psum_tensor(name, shape, dt))

    def sem(name):
        return ctx.enter_context(nc.semaphore(name))

    return sb, psum, sem


def project_inputs(nc, a, scanT_dram, nat_dram, scalars):
    with ExitStack() as ctx:
        sb, psum, sem = allocators(nc, ctx)
        xT = sb("xT", [P, KC, SEQ], F32)
        w_low = sb("w_low", [P, KC, 2, RANK], F32)
        w_tr = [sb(f"w_tr{i}", [P, KC, P], F32) for i in range(2)]
        w_nat = [sb(f"w_nat{i}", [P, KC, 512], F32) for i in range(2)]
        wg2 = sb("wg2", [RANK, GLA_BLOCKS * P], F32)
        small_cols = sb("small_cols", [P, GLA_BLOCKS + 5 * XBC_BLOCKS], F32)
        small_rows = sb("small_rows", [P, 2, HEADS_SSD], F32)
        tri = sb("tri1", [P, P], F32)
        ones = sb("ones1", [P, P], F32)
        carry = sb("carry", [P, SEQ], F32)
        low = sb("low", [RANK, SEQ], F32)
        stage = [sb(f"stage{i}", [P, SEQ], F32) for i in range(2)]
        padded = [sb(f"padded{i}", [P, SEQ + CONV - 1], F32) for i in range(2)]
        conv = [sb(f"conv{i}", [P, SEQ], F32) for i in range(2)]
        dt_tmp = sb("dt_tmp", [P, 3, TILES * HEADS_SSD], F32)
        a_neg = sb("a_neg", [P, HEADS_SSD], F32)
        a_all = sb("a_all", [P, TILES * HEADS_SSD], F32)
        group = [psum(f"group{i}", [P, 1024], F32) for i in range(4)]
        low_ps, dt_ps = group[2], group[3]

        given = sem("given1")
        x_loaded = sem("x_loaded")
        tr_loaded = [sem(f"tr_loaded{i}") for i in range(2)]
        nat_loaded = [sem(f"nat_loaded{i}") for i in range(2)]
        low_made, low_ready, dt_made = sem("low_made"), sem("low_ready"), sem("dt_made")
        gate_made, gate_read = sem("gate_made"), sem("gate_read")
        tr_made, tr_read, tr_used = sem("tr_made"), sem("tr_read"), sem("tr_used")
        nat_made, nat_read = sem("nat_made"), sem("nat_read")
        staged = sem("staged")
        stored = [sem(f"stored{i}") for i in range(2)]
        conv_done = sem("conv_done")
        consts_made = sem("consts1_made")
        act_step, dve_step = sem("act1_step"), sem("dve1_step")
        dt_biased, dt_logged, a_ready, cs_made = sem("dt_biased"), sem("dt_logged"), sem("a_ready"), sem("cs_made")
        cs_exp_in, cs_exp_out = sem("cs_exp_in"), sem("cs_exp_out")
        gate_min, gate_log, gate_sum = sem("gate_min"), sem("gate_log"), sem("gate_sum")
        scal_done = sem("scal_done")

        NQK = 2 * GLA_BLOCKS
        NTR = NQK + XBC_BLOCKS
        taps = small_cols[:, GLA_BLOCKS:GLA_BLOCKS + CONV * XBC_BLOCKS]
        NG, PAIRS = GLA_BLOCKS, TILES // 2

        with nc.Block() as block:
            @block.sync
            def _(sp):
                sp.dma_start(w_low[:, :, :, :], a["w_low"]).then_inc(given, 16)
                sp.dma_start(xT[:, :, :], a["xT"]).then_inc(x_loaded, 16)
                sp.dma_start(wg2[:, :], a["wg2"]).then_inc(given, 16)
                sp.dma_start(small_cols[:, :], a["small_cols"]).then_inc(given, 16)
                sp.dma_start(small_rows[:, :, :], a["small_rows"]).then_inc(given, 16)
                sp.dma_start(tri[:, :], a["tri"]).then_inc(given, 16)
                for j in range(2):
                    sp.dma_start(w_tr[j][:, :, :], a["w_tr"][j]).then_inc(tr_loaded[j], 16)
                for j in range(2):
                    sp.dma_start(w_nat[j][:, :, :], a["w_nat"][j]).then_inc(nat_loaded[j], 16)

                def store(dst, src_slot, count):
                    sp.wait_ge(staged, count + 1)
                    sp.dma_start(dst, stage[src_slot][:, :]).then_inc(stored[src_slot], 16)

                for g in range(NG):
                    store(scanT_dram[NTR + g], g % 2, g)
                with sp.Fori(0, NTR // 2 - 1) as i:
                    for j in range(2):
                        sp.wait_ge(tr_made, 2 * i + j + 1)
                        sp.dma_start(w_tr[j][:, :, :], a["w_tr"][2 * i + 2 + j]).then_inc(tr_loaded[j], 16)
                        store(scanT_dram[2 * i + j], j, NG + 2 * i + j)
                for j in range(2):
                    store(scanT_dram[NTR - 2 + j], j, NG + NTR - 2 + j)

                def pairs(kind, half):
                    for q in range(PAIRS):
                        count = NG + NTR + (2 * kind + half) * PAIRS + q
                        sp.wait_ge(staged, count + 1)
                        for e in range(2):
                            sp.dma_start(nat_dram[kind, 2 * q + e, :, half * 512:(half + 1) * 512],
                                         stage[q % 2][:, e * 512:(e + 1) * 512]).then_inc(stored[q % 2], 16)

                with sp.Fori(0, 2) as kind:
                    for half in range(2):
                        pairs(kind, half)
                        sp.wait_ge(nat_made, (2 * kind + half + 1) * PAIRS)
                        sp.dma_start(w_nat[half][:, :, :], a["w_nat"][2 * kind + 2 + half]
                                     ).then_inc(nat_loaded[half], 16)
                for half in range(2):
                    pairs(2, half)
                for j in range(2):
                    sp.wait_ge(stored[j], 16 * ((NG + NTR) // 2 + 2 * 6 * PAIRS // 2))

            @block.tensor
            def _(pe):
                pe.wait_ge(given, 80)
                pe.wait_ge(x_loaded, 16)
                for c in range(2):
                    for k in range(KC):
                        last = pe.matmul(low_ps[0:RANK, c * 512:(c + 1) * 512], w_low[:, k, 0, :],
                                         xT[:, k, c * 512:(c + 1) * 512], start=(k == 0), stop=(k == KC - 1))
                last.then_inc(low_made, 1)
                for t in range(TILES):
                    for k in range(KC):
                        last = pe.matmul(dt_ps[:, t * RANK:(t + 1) * RANK], xT[:, k, t * P:(t + 1) * P],
                                         w_low[:, k, 1, :], start=(k == 0), stop=(k == KC - 1))
                last.then_inc(dt_made, 1)

                def transposed(i, j):
                    pe.wait_ge(tr_loaded[j], 16 * (i + 1))
                    if not (isinstance(i, int) and i == 0):
                        pe.wait_ge(tr_read, 2 * i + j - 1)
                    for c in range(2):
                        for k in range(KC):
                            last = pe.matmul(group[j][:, c * 512:(c + 1) * 512], w_tr[j][:, k, :],
                                             xT[:, k, c * 512:(c + 1) * 512], start=(k == 0), stop=(k == KC - 1))
                    last.then_inc(tr_made, 1)

                for j in range(2):
                    transposed(0, j)
                pe.wait_ge(a_ready, 1)
                pe.wait_ge(consts_made, 4)
                pe.matmul(dt_ps[:, 512:512 + P], tri[:, :], a_all[:, :], start=True, stop=True)
                pe.matmul(dt_ps[:, 512 + P:512 + 2 * P], ones[:, :], a_all[:, :], start=True,
                          stop=True).then_inc(cs_made, 1)
                pe.wait_ge(low_ready, 1)
                for g in range(NG):
                    if g >= 1:
                        pe.wait_ge(gate_read, g)
                    for c in range(2):
                        last = pe.matmul(low_ps[:, c * 512:(c + 1) * 512], wg2[:, g * P:(g + 1) * P],
                                         low[:, c * 512:(c + 1) * 512], start=True, stop=True)
                    last.then_inc(gate_made, 1)
                with pe.Fori(1, NTR // 2) as i:
                    for j in range(2):
                        transposed(i, j)

                def natural(kind, half):
                    pe.wait_ge(nat_loaded[half], 16 * (kind + 1))
                    for q in range(PAIRS):
                        count = (2 * kind + half) * PAIRS + q
                        if isinstance(count, int) and count < 2:
                            pe.wait_ge(tr_read, NTR)
                        else:
                            pe.wait_ge(nat_read, count - 1)
                        for e in range(2):
                            for k in range(KC):
                                last = pe.matmul(group[q % 2][:, e * 512:(e + 1) * 512],
                                                 xT[:, k, (2 * q + e) * P:(2 * q + e + 1) * P],
                                                 w_nat[half][:, k, :], start=(k == 0), stop=(k == KC - 1))
                        last.then_inc(nat_made, 1)

                for half in range(2):
                    natural(0, half)
                with pe.Fori(1, 3) as kind:
                    for half in range(2):
                        natural(kind, half)

            @block.scalar
            def _(act):
                act.wait_ge(given, 80)
                act.activation(a_neg[:, :], small_rows[:, 1, :], ACT.Exp).then_inc(act_step, 1)
                act.wait_ge(low_made, 1)
                act.activation(low[:, :], low_ps[0:RANK, :], ACT.Copy).then_inc(low_ready, 1)
                act.wait_ge(dt_biased, 1)
                act.activation(dt_tmp[:, 1, :], dt_tmp[:, 0, :], ACT.Abs).then_inc(act_step, 1)
                act.wait_ge(act_step, 2)
                act.activation(dt_tmp[:, 1, :], dt_tmp[:, 1, :], ACT.Exp, scale=-1.0).then_inc(act_step, 1)
                act.wait_ge(act_step, 3)
                act.activation(dt_tmp[:, 1, :], dt_tmp[:, 1, :], ACT.Ln, bias=1.0).then_inc(dt_logged, 1)
                for g in range(NG):
                    act.wait_ge(gate_min, g + 1)
                    if g >= 2:
                        act.wait_ge(gate_sum, g - 1)
                    act.activation(conv[g % 2][:, :], low_ps[:, :], ACT.Abs,
                                   bias=small_cols[:, g:g + 1]).then_inc(act_step, 1)
                    act.wait_ge(act_step, 4 + 3 * g)
                    act.activation(conv[g % 2][:, :], conv[g % 2][:, :], ACT.Exp, scale=-1.0).then_inc(act_step, 1)
                    act.wait_ge(act_step, 5 + 3 * g)
                    act.activation(conv[g % 2][:, :], conv[g % 2][:, :], ACT.Ln, bias=1.0).then_inc(gate_log, 1)
                    act.wait_ge(gate_sum, g + 1)
                    if g >= 2:
                        act.wait_ge(stored[g % 2], 16 * (g // 2))
                    act.activation(stage[g % 2][:, :], padded[g % 2][:, CONV - 1:], ACT.Copy,
                                   scale=1.0 / GATE_TAU).then_inc(staged, 1)
                    act.wait_ge(staged, g + 1)
                    act.sem_inc(act_step, 1)
                act.wait_ge(cs_exp_in, 1)
                for what in (3, 4, 5):
                    last = act.activation(scalars[:, :, what, :], scalars[:, :, what, :], ACT.Exp)
                last.then_inc(cs_exp_out, 1)

                def copy_out(i, j, scale):
                    act.wait_ge(tr_made, 2 * i + j + 1)
                    act.wait_ge(stored[j], 16 * (NG // 2 + i))
                    act.activation(stage[j][:, :], group[j][:, :], ACT.Copy, scale=scale).then_inc(staged, 1)
                    act.wait_ge(staged, NG + 2 * i + j + 1)
                    act.sem_inc(tr_read, 1)

                with act.Fori(0, GLA_BLOCKS // 2) as i:
                    for j in range(2):
                        copy_out(i, j, Q_SCALE)
                with act.Fori(GLA_BLOCKS // 2, GLA_BLOCKS) as i:
                    for j in range(2):
                        copy_out(i, j, 1.0)

                def convolved(i, j):
                    b = 2 * i + j
                    act.wait_ge(tr_made, NQK + b + 1)
                    act.activation(padded[j][:, CONV - 1:], group[j][:, :], ACT.Copy).then_inc(tr_read, 1)
                    act.wait_ge(conv_done, b + 1)
                    act.wait_ge(stored[j], 16 * ((NG + NQK) // 2 + i))
                    act.activation(stage[j][:, :], conv[j][:, :], ACT.Silu).then_inc(staged, 1)

                with act.Fori(0, XBC_BLOCKS // 2) as i:
                    for j in range(2):
                        convolved(i, j)

                def natural(kind, half, func):
                    for q in range(PAIRS):
                        count = (2 * kind + half) * PAIRS + q
                        act.wait_ge(nat_made, count + 1)
                        act.wait_ge(stored[q % 2], 16 * ((NG + NTR) // 2) + 32 * ((2 * kind + half) * (PAIRS // 2) + q // 2))
                        act.activation(stage[q % 2][:, :], group[q % 2][:, :], func).then_inc(staged, 1)
                        act.wait_ge(staged, NG + NTR + count + 1)
                        act.sem_inc(nat_read, 1)

                for half in range(2):
                    natural(0, half, ACT.Copy)
                with act.Fori(1, 3) as kind:
                    for half in range(2):
                        natural(kind, half, ACT.Silu)

            @block.vector
            def _(dve):
                dve.memset(ones[:, :], 1.0).then_inc(consts_made, 1)
                dve.memset(carry[:, :], 1.0).then_inc(dve_step, 1)
                dve.wait_ge(dve_step, 1)
                dve.memset(carry[:, :].rearrange("p (t u) -> p t u", u=P)[:, :, 0:1], 0.0).then_inc(consts_made, 1)
                for j in range(2):
                    dve.memset(padded[j][:, 0:CONV - 1], 0.0).then_inc(consts_made, 1)
                dve.wait_ge(consts_made, 4)
                dve.wait_ge(given, 80)
                dve.wait_ge(dt_made, 1)
                z3 = "p (t h) -> p t h"

                def per_head(row):
                    return row.unsqueeze(1).to_broadcast([P, TILES, HEADS_SSD])

                dve.tensor_tensor(dt_tmp[:, 0, :].rearrange(z3, h=HEADS_SSD),
                                  dt_ps[:, 0:TILES * HEADS_SSD].rearrange(z3, h=HEADS_SSD),
                                  per_head(small_rows[:, 0, :]), ALU.add).then_inc(dt_biased, 1)
                dve.wait_ge(dt_logged, 1)
                dve.wait_ge(dt_biased, 1)
                dve.scalar_tensor_tensor(dt_tmp[:, 2, :], dt_tmp[:, 0, :], 0.0, dt_tmp[:, 1, :], ALU.max,
                                         ALU.add).then_inc(dve_step, 1)
                dve.wait_ge(dve_step, 2)
                dt3 = dt_tmp[:, 2, :].rearrange(z3, h=HEADS_SSD)
                dve.tensor_copy(scalars[:, :, 1, :], dt3)
                dve.wait_ge(act_step, 1)
                dve.scalar_tensor_tensor(a_all[:, :].rearrange(z3, h=HEADS_SSD), dt3, -1.0,
                                         per_head(a_neg[:, :]), ALU.mult, ALU.mult).then_inc(a_ready, 1)
                dve.wait_ge(a_ready, 1)
                dve.tensor_copy(scalars[:, :, 0, :], a_all[:, :].rearrange(z3, h=HEADS_SSD))
                dve.wait_ge(cs_made, 1)
                cs = dt_ps[:, 512:512 + P].rearrange(z3, h=HEADS_SSD)
                total = dt_ps[:, 512 + P:512 + 2 * P].rearrange(z3, h=HEADS_SSD)
                dve.tensor_scalar(scalars[:, :, 2, :], cs, -1.0, None, ALU.mult)
                dve.tensor_copy(scalars[:, :, 3, :], cs)
                dve.tensor_copy(scalars[:, :, 5, :], total).then_inc(dve_step, 1)
                dve.wait_ge(dve_step, 3)
                dve.tensor_tensor(scalars[:, :, 4, :], scalars[:, :, 5, :], cs, ALU.subtract).then_inc(cs_exp_in, 1)
                for g in range(NG):
                    dve.wait_ge(gate_made, g + 1)
                    if g >= 2:
                        dve.wait_ge(staged, g - 1)
                    t = padded[g % 2][:, CONV - 1:]
                    dve.tensor_scalar(t, low_ps[:, :], small_cols[:, g:g + 1], 0.0, ALU.add, ALU.min).then_inc(gate_min, 1)
                    dve.wait_ge(gate_min, g + 1)
                    dve.wait_ge(gate_log, g + 1)
                    dve.tensor_tensor(t, t, conv[g % 2][:, :], ALU.subtract).then_inc(gate_read, 1)
                    dve.wait_ge(gate_read, g + 1)
                    dve.tensor_tensor_scan(t, carry[:, :], t, 0.0, ALU.mult, ALU.add).then_inc(gate_sum, 1)
                dve.wait_ge(cs_exp_out, 1)
                dve.tensor_tensor(scalars[:, :, 4, :], scalars[:, :, 4, :], scalars[:, :, 1, :],
                                  ALU.mult).then_inc(scal_done, 1)
                dve.wait_ge(staged, NG)

                for b in range(XBC_BLOCKS):
                    j = b % 2
                    dve.wait_ge(tr_read, NQK + b + 1)
                    if b >= 2:
                        dve.wait_ge(staged, NG + NQK + b - 1)
                    dve.tensor_scalar(conv[j][:, :], padded[j][:, 0:SEQ], taps[:, CONV * b:CONV * b + 1],
                                      small_cols[:, GLA_BLOCKS + CONV * XBC_BLOCKS + b:GLA_BLOCKS + CONV * XBC_BLOCKS + b + 1],
                                      ALU.mult, ALU.add).then_inc(dve_step, 1)
                    for tap in range(1, CONV):
                        dve.wait_ge(dve_step, 3 + 3 * b + tap)
                        last = dve.scalar_tensor_tensor(conv[j][:, :], padded[j][:, tap:tap + SEQ],
                                                        taps[:, CONV * b + tap:CONV * b + tap + 1],
                                                        conv[j][:, :], ALU.mult, ALU.add)
                        last.then_inc(dve_step if tap < CONV - 1 else conv_done, 1)


def mix_tokens(nc, a, scanT_dram, nat_dram, scalars, h1_dram):
    with ExitStack() as ctx:
        sb, psum, sem = allocators(nc, ctx)
        w_out = sb("w_out", [P, 2 * KC, D], F32)
        ident = sb("ident2", [P, P], F32)
        tri = sb("tri2", [P, P], F32)
        ident16 = sb("ident16", [P, P], BF16)
        future16 = sb("future16", [P, P], BF16)
        level_mask = sb("level_mask", [P, LEVELS + 1, P], BF16)
        gainT = sb("gainT", [P, 2 * KC], F32)
        d_row = sb("d_row", [P, HEADS_SSD], F32)
        ln = sb("ln_rows1", [P, 2, D], F32)
        eps = sb("eps2", [P, 2], F32)
        qkb = sb("qkb", [P, 3, GLA_BLOCKS * P], F32)
        xsb = sb("xsb", [P, KC + 1, P], F32)
        cT = sb("cT", [P, 2, P], F32)
        v_in = sb("v_in", [P, D], F32)
        gate_in = sb("gate_in", [P, 2, D], F32)
        x_in = sb("x_in", [P, D], F32)
        expo = sb("expo", [P, LEVELS, GLA_BLOCKS * P], F32)
        q_lv = sb("q_lv", [P, LEVELS, GLA_BLOCKS * P], F32)
        k_lv = sb("k_lv", [P, LEVELS, GLA_BLOCKS * P], F32)
        q_in = sb("q_in", [P, GLA_BLOCKS * P], F32)
        k_end = sb("k_end", [P, GLA_BLOCKS * P], F32)
        exp_b = sb("exp_b", [P, GLA_BLOCKS * P], F32)
        exp_end = sb("exp_end", [P, GLA_BLOCKS * P], F32)
        b_last = sb("b_last", [P, 2, GLA_BLOCKS], F32)
        kb_nat = sb("kb_nat", [P, (GLA_BLOCKS + 1) * P], F32)
        masked = sb("masked", [P, (LEVELS + 1) * P], F32)
        att = sb("att", [P, GLA_BLOCKS, P], F32)
        state = sb("gla_state", [P, D], F32)
        hstate = sb("ssd_state", [P, 512], F32)
        scal = sb("scal", [P, 2, KINDS, HEADS_SSD], F32)
        xs = sb("xs", [P, D], F32)
        xdt = sb("xdt", [P, D], F32)
        xend = sb("xend", [P, D], F32)
        decay = sb("decay", [P, HEADS_SSD, P], F32)
        o_sb = sb("o_sb", [P, D], F32)
        y_sb = sb("y_sb", [P, D], F32)
        mixT = sb("mixT", [P, 2 * KC, P], F32)
        stats = sb("stats1", [P, 2, 6], F32)
        moments = sb("moments1", [P, 2], F32)
        lstd = sb("lstd", [P, 2], F32)
        ms = sb("ms", [P, 3, 8], F32)
        bank = [psum(f"mix_bank{i}", [P, D], F32) for i in range(4)]
        A, B, C, Dk = bank
        place = dict(X=A, L0=B, L1=C, KB=Dk, L2=A, L3=B, CB=C, CS0=Dk, CS1=A, OTa=B, OTb=Dk, OUT=B,
                     O=A, SN=Dk, YO=A, YD=C, HN=Dk)
        made = {k: sem(f"made_{k}") for k in place}
        read = {k: sem(f"read_{k}") for k in place}
        consts = sem("consts2")
        wout_loaded = sem("wout_loaded")
        zeros_made, eps_made = sem("zeros_made"), sem("eps2_made")
        qkb_loaded, xsb_loaded, v_loaded, gate_loaded, x_loaded = (
            sem("qkb_loaded"), sem("xsb_loaded"), sem("v_loaded"), sem("gate_loaded"), sem("x2_loaded"))
        cT_loaded = [sem(f"cT_loaded{i}") for i in range(2)]
        scal_ready = sem("scal_ready")
        expo_in, expo_out, levels_ready = sem("expo_in"), sem("expo_out"), sem("levels_ready")
        prep_step, dve_step, act_step = sem("prep_step"), sem("dve2_step"), sem("act2_step")
        xdt_ready, decay_ready, skip_ready = sem("xdt_ready"), sem("decay_ready"), sem("skip_ready")
        o_root, y_root, y_gated, og_ready, yg_ready = (
            sem("o_root"), sem("y_root"), sem("y_gated"), sem("og_ready"), sem("yg_ready"))
        state_ready, hstate_ready = sem("state_ready"), sem("hstate_ready")
        var_ready, root_ready, h1_ready, h1_stored = sem("var1"), sem("root1"), sem("h1_ready2"), sem("h1_stored")
        passed, sp_passed = sem("dve2_waits_passed"), sem("sp2_waits_passed")
        att_ready = sem("att_ready")
        norm_step = sem("norm1_step")
        CONSTS = 8 * 16
        skip = masked

        def tiles(engine, body):
            body(0, 0)
            with engine.Fori(0, (TILES - 2) // 2) as i:
                body(2 * i + 1, 1)
                body(2 * i + 2, 0)
            body(TILES - 1, 1)

        def first(t):
            return isinstance(t, int) and t == 0

        def final(t):
            return isinstance(t, int) and t == TILES - 1

        with nc.Block() as block:
            @block.sync
            def _(sp):
                def load_qkb(t):
                    for w, b0 in enumerate((0, GLA_BLOCKS, 2 * GLA_BLOCKS + XBC_BLOCKS)):
                        sp.dma_start(qkb[:, w, :].rearrange("p (b u) -> p b u", u=P),
                                     scanT_dram[b0:b0 + GLA_BLOCKS, :, bass.ts(t, P)].rearrange("b p u -> p b u")
                                     ).then_inc(qkb_loaded, 16)

                def load_xsb(t):
                    b0 = 2 * GLA_BLOCKS
                    sp.dma_start(xsb[:, :, :], scanT_dram[b0:b0 + KC + 1, :, bass.ts(t, P)].rearrange("b p u -> p b u")
                                 ).then_inc(xsb_loaded, 16)

                def load_cT(t, s):
                    sp.dma_start(cT[:, s, :], scanT_dram[2 * GLA_BLOCKS + KC + 1, :, bass.ts(t, P)]
                                 ).then_inc(cT_loaded[s], 16)

                def load_v(t):
                    sp.dma_start(v_in[:, :], nat_dram[0, t]).then_inc(v_loaded, 16)

                def load_gates(t):
                    for g in range(2):
                        sp.dma_start(gate_in[:, g, :], nat_dram[1 + g, t]).then_inc(gate_loaded, 16)

                def load_x(t):
                    sp.dma_start(x_in[:, :], a["x"][t]).then_inc(x_loaded, 16)

                load_qkb(0)
                load_xsb(0)
                load_cT(0, 0)
                load_v(0)
                for dst, name in ((ident[:, :], "ident"), (tri[:, :], "tri"), (ident16[:, :], "ident16"), (future16[:, :], "future16"),
                                  (level_mask[:, :, :], "level_mask"), (gainT[:, :], "gainT"),
                                  (d_row[:, :], "d_row"), (ln[:, :, :], "ln1")):
                    sp.dma_start(dst, a[name]).then_inc(consts, 16)
                load_gates(0)
                load_x(0)
                sp.dma_start(w_out[:, :, :], a["w_out"]).then_inc(wout_loaded, 16)

                def body(t, s):
                    if not final(t):
                        sp.wait_ge(made["CB"], t + 1)
                        load_xsb(t + 1)
                        sp.wait_ge(made["L3"], t + 1)
                        sp.sem_inc(sp_passed, 1)
                        load_qkb(t + 1)
                        load_cT(t + 1, 1 - s)
                    if not first(t):
                        sp.wait_ge(h1_ready, t)
                        sp.dma_start(h1_dram[t - 1], x_in[:, :]).then_inc(h1_stored, 16)
                        sp.wait_ge(h1_stored, 16 * t)
                        load_x(t)
                    if not final(t):
                        sp.wait_ge(made["SN"], t + 1)
                        load_v(t + 1)
                        sp.wait_ge(yg_ready, t + 1)
                        load_gates(t + 1)

                tiles(sp, body)
                sp.wait_ge(h1_ready, TILES)
                sp.dma_start(h1_dram[TILES - 1], x_in[:, :]).then_inc(h1_stored, 16)
                sp.wait_ge(h1_stored, 16 * TILES)

            @block.tensor
            def _(pe):
                pe.wait_ge(consts, CONSTS)
                pe.wait_ge(zeros_made, 4)

                def out_of(t):
                    for part, src, ready in (("OTa", o_sb, og_ready), ("OTb", y_sb, yg_ready)):
                        if final(t):
                            pe.wait_ge(read["OUT" if part == "OTa" else "HN"], TILES)
                        else:
                            pe.wait_ge(read["L3" if part == "OTa" else "CS0"], t + 2)
                        pe.wait_ge(ready, t + 1)
                        for k in range(KC):
                            last = pe.transpose(place[part][:, k * P:(k + 1) * P], src[:, k * P:(k + 1) * P],
                                                ident[:, :])
                        last.then_inc(made[part], 1)
                    pe.wait_ge(read["OTa"], t + 1)
                    pe.wait_ge(read["OTb"], t + 1)
                    for c in range(2):
                        for k in range(2 * KC):
                            last = pe.matmul(place["OUT"][:, c * 512:(c + 1) * 512], mixT[:, k, :],
                                             w_out[:, k, c * 512:(c + 1) * 512], start=(k == 0), stop=(k == 2 * KC - 1))
                    last.then_inc(made["OUT"], 1)

                def levels(t, h):
                    part = f"L{h}"
                    cols = slice(h * P, (h + 1) * P)
                    for lv in range(LEVELS + 1):
                        kk = k_lv[:, lv, cols] if lv < LEVELS else qkb[:, 1, cols]
                        qq = q_lv[:, lv, cols] if lv < LEVELS else qkb[:, 0, cols]
                        last = pe.matmul(place[part][:, lv * P:(lv + 1) * P], kk, qq, start=True, stop=True)
                    last.then_inc(made[part], 1)

                def body(t, s):
                    pe.wait_ge(xsb_loaded, 16 * (t + 1))
                    if not first(t):
                        pe.wait_ge(read["YO"], t)
                    for k in range(KC):
                        last = pe.transpose(place["X"][:, k * P:(k + 1) * P], xsb[:, k, :], ident[:, :])
                    last.then_inc(made["X"], 1)
                    pe.wait_ge(levels_ready, t + 1)
                    if not first(t):
                        pe.wait_ge(read["OUT"], t)
                        pe.wait_ge(read["YD"], t)
                        pe.wait_ge(read["HN"], t)
                    levels(t, 0)
                    levels(t, 1)
                    for h in range(GLA_BLOCKS):
                        pe.transpose(place["KB"][:, h * P:(h + 1) * P], k_end[:, h * P:(h + 1) * P], ident[:, :])
                    pe.transpose(place["KB"][:, 512:512 + P], xsb[:, KC, :], ident[:, :]).then_inc(made["KB"], 1)
                    pe.wait_ge(read["X"], t + 1)
                    levels(t, 2)
                    pe.wait_ge(read["L0"], t + 1)
                    levels(t, 3)
                    pe.wait_ge(read["L1"], t + 1)
                    pe.wait_ge(cT_loaded[s], 8 * (t - s) + 16)
                    for g in range(2):
                        rows = slice(64 * g, 64 * g + 64)
                        last = pe.matmul(place["CB"][:, g * 512:g * 512 + P], xsb[rows, KC, :], cT[rows, s, :],
                                         start=True, stop=True)
                    last.then_inc(made["CB"], 1)
                    pe.wait_ge(scal_ready, t + 1)
                    for g in range(2):
                        part = f"CS{g}"
                        pe.wait_ge(read["KB"] if g == 0 else read["L2"], t + 1)
                        for c in range(2):
                            pe.matmul(place[part][:, c * 512:(c + 1) * 512], ident16[:, :],
                                      future16[:, :].unsqueeze(1).to_broadcast([P, 4, P]),
                                      start=True, stop=False, skip_group_check=True)
                            for q in range(4):
                                h = 8 * g + 4 * c + q
                                last = pe.matmul(place[part][:, c * 512 + q * P:c * 512 + (q + 1) * P],
                                                 scal[:, s, 0, h:h + 1].to_broadcast([P, P]), tri[:, :],
                                                 start=False, stop=(q == 3), skip_group_check=True)
                        last.then_inc(made[part], 1)
                    if not first(t):
                        out_of(t - 1)
                    pe.wait_ge(read["CS1"], t + 1)
                    pe.wait_ge(att_ready, GLA_BLOCKS * (t + 1))
                    pe.wait_ge(v_loaded, 16 * (t + 1))
                    if not first(t):
                        pe.wait_ge(state_ready, t)
                    for h in range(GLA_BLOCKS):
                        e = slice(h * 256, (h + 1) * 256)
                        pe.matmul(place["O"][:, e], q_in[:, h * P:(h + 1) * P], state[:, e], start=True, stop=False)
                        last = pe.matmul(place["O"][:, e], att[:, h, :], v_in[:, e], start=False, stop=True)
                    last.then_inc(made["O"], 1)
                    if not first(t):
                        pe.wait_ge(read["OTb"], t)
                    else:
                        pe.wait_ge(read["CS0"], 1)
                    for h in range(GLA_BLOCKS):
                        e = slice(h * 256, (h + 1) * 256)
                        last = pe.matmul(place["SN"][:, e], kb_nat[:, h * P:(h + 1) * P], v_in[:, e],
                                         start=True, stop=True)
                    last.then_inc(made["SN"], 1)
                    pe.wait_ge(decay_ready, t + 1)
                    pe.wait_ge(skip_ready, t + 1)
                    for c in range(2):
                        pe.matmul(place["YD"][:, c * 512:(c + 1) * 512], ident[:, :], skip[:, c * 512:(c + 1) * 512],
                                  start=True, stop=False, skip_group_check=True)
                        for q in range(8):
                            h = 8 * c + q
                            last = pe.matmul(place["YD"][:, h * 64:(h + 1) * 64], decay[:, h, :],
                                             xdt[:, h * 64:(h + 1) * 64], start=False, stop=(q == 7),
                                             skip_group_check=True)
                    last.then_inc(made["YD"], 1)
                    pe.wait_ge(read["O"], t + 1)
                    if not first(t):
                        pe.wait_ge(hstate_ready, t)
                    for g in range(2):
                        rows = slice(64 * g, 64 * g + 64)
                        last = pe.matmul(place["YO"][:, g * 512:(g + 1) * 512], cT[rows, s, :], hstate[rows, :],
                                         start=True, stop=True)
                    last.then_inc(made["YO"], 1)
                    pe.wait_ge(read["SN"], t + 1)
                    for g in range(2):
                        last = pe.matmul(place["HN"][:, g * 512:(g + 1) * 512], kb_nat[:, 512:512 + P],
                                         xend[:, g * 512:(g + 1) * 512], start=True, stop=True)
                    last.then_inc(made["HN"], 1)

                tiles(pe, body)
                pe.wait_ge(wout_loaded, 16)
                out_of(TILES - 1)

            @block.scalar
            def _(act):
                act.wait_ge(consts, CONSTS)
                act.wait_ge(eps_made, 2)

                def exponentials(t, s):
                    act.wait_ge(expo_in, t + 1)
                    act.activation(expo[:, :, :].rearrange("p l u -> p (l u)"),
                                   expo[:, :, :].rearrange("p l u -> p (l u)"), ACT.Exp)
                    act.activation(exp_end[:, :], exp_end[:, :], ACT.Exp)
                    act.activation(exp_b[:, :], qkb[:, 2, :], ACT.Exp)
                    act.activation(b_last[:, s, :], qkb[:, 2, :].rearrange("p (h u) -> p h u", u=P)[:, :, P - 1],
                                   ACT.Exp).then_inc(expo_out, 1)

                def body(t, s):
                    act.wait_ge(made["X"], t + 1)
                    if not first(t):
                        act.wait_ge(skip_ready, t)
                    act.activation(xs[:, :], place["X"][:, :], ACT.Copy).then_inc(read["X"], 1)
                    act.wait_ge(made["KB"], t + 1)
                    if not first(t):
                        act.wait_ge(made["HN"], t)
                    act.activation(kb_nat[:, :], place["KB"][:, 0:5 * P], ACT.Copy).then_inc(read["KB"], 1)
                    act.wait_ge(scal_ready, t + 1)
                    for g in range(2):
                        part = f"CS{g}"
                        act.wait_ge(made[part], t + 1)
                        for q in range(8):
                            h = 8 * g + q
                            last = act.activation(decay[:, h, :], place[part][:, q * P:(q + 1) * P], ACT.Exp,
                                                  bias=scal[:, s, 2, h:h + 1])
                        last.then_inc(read[part], 1)
                    if not first(t):
                        transposed_out(t)
                        root_of_norm(t)
                    if not final(t):
                        exponentials(t + 1, 1 - s)
                    act.wait_ge(made["O"], t + 1)
                    for h in range(GLA_BLOCKS):
                        e = slice(h * 256, (h + 1) * 256)
                        last = act.activation(o_sb[:, e], place["O"][:, e], ACT.Square, accum_out=ms[:, 0, h:h + 1])
                    last.then_inc(act_step, 1)
                    act.wait_ge(act_step, 2 * t + 1)
                    act.activation(ms[:, 1, 0:4], ms[:, 0, 0:4], ACT.Sqrt, scale=1.0 / 256,
                                   bias=eps[:, 1:2]).then_inc(o_root, 1)
                    act.wait_ge(y_gated, t + 1)
                    for g in range(2):
                        e = slice(g * 512, (g + 1) * 512)
                        last = act.activation(xs[:, e], y_sb[:, e], ACT.Square, accum_out=ms[:, 0, 4 + g:5 + g])
                    last.then_inc(act_step, 1)
                    act.wait_ge(act_step, 2 * t + 2)
                    act.activation(ms[:, 1, 4:6], ms[:, 0, 4:6], ACT.Sqrt, scale=1.0 / 512,
                                   bias=eps[:, 1:2]).then_inc(y_root, 1)

                def transposed_out(t):
                    for j, part in enumerate(("OTa", "OTb")):
                        act.wait_ge(made[part], t)
                        for k in range(KC):
                            last = act.activation(mixT[:, KC * j + k, :], place[part][:, k * P:(k + 1) * P],
                                                  ACT.Copy, scale=gainT[:, KC * j + k:KC * j + k + 1])
                        last.then_inc(read[part], 1)

                def root_of_norm(t):
                    act.wait_ge(var_ready, t)
                    act.activation(lstd[:, 0:1], moments[:, 1:2], ACT.Sqrt, bias=eps[:, 0:1]).then_inc(root_ready, 1)

                exponentials(0, 0)
                tiles(act, body)
                transposed_out(TILES)
                root_of_norm(TILES)

            @block.vector
            def _(dve):
                for t, n in ((q_lv, 0), (k_lv, 1)):
                    dve.memset(t[:, :, :], 0.0).then_inc(zeros_made, 1)
                dve.memset(state[:, :], 0.0).then_inc(zeros_made, 1)
                dve.memset(hstate[:, :], 0.0).then_inc(zeros_made, 1)
                dve.memset(eps[:, 0:1], LN_EPS).then_inc(eps_made, 1)
                dve.memset(eps[:, 1:2], RMS_EPS).then_inc(eps_made, 1)
                dve.sem_inc(read["OUT"], 1)
                dve.wait_ge(zeros_made, 4)
                dve.wait_ge(consts, CONSTS)

                def pairs(x, lv):
                    return x.rearrange("p (n two m) -> p n two m", two=2, m=1 << lv)

                def exponents(t):
                    dve.wait_ge(qkb_loaded, 48 * (t + 1))
                    for lv in range(LEVELS):
                        b, e = pairs(qkb[:, 2, :], lv), pairs(expo[:, lv, :], lv)
                        m = 1 << lv
                        ref = b[:, :, 0, m - 1:m].to_broadcast([P, GLA_BLOCKS * P // (2 * m), m])
                        dve.tensor_tensor(e[:, :, 0, :], ref, b[:, :, 0, :], ALU.subtract)
                        dve.tensor_tensor(e[:, :, 1, :], b[:, :, 1, :], ref, ALU.subtract)
                    b = qkb[:, 2, :].rearrange("p (h u) -> p h u", u=P)
                    dve.tensor_tensor(exp_end[:, :].rearrange("p (h u) -> p h u", u=P),
                                      b[:, :, P - 1:P].to_broadcast([P, GLA_BLOCKS, P]), b,
                                      ALU.subtract).then_inc(expo_in, 1)

                def level_operands(t):
                    dve.wait_ge(expo_out, t + 1)
                    if not first(t):
                        dve.wait_ge(made["O"], t)
                    for lv in range(LEVELS):
                        e = pairs(expo[:, lv, :], lv)
                        dve.tensor_tensor(pairs(q_lv[:, lv, :], lv)[:, :, 1, :], pairs(qkb[:, 0, :], lv)[:, :, 1, :],
                                          e[:, :, 1, :], ALU.mult)
                        dve.tensor_tensor(pairs(k_lv[:, lv, :], lv)[:, :, 0, :], pairs(qkb[:, 1, :], lv)[:, :, 0, :],
                                          e[:, :, 0, :], ALU.mult)
                    dve.tensor_tensor(q_in[:, :], qkb[:, 0, :], exp_b[:, :], ALU.mult)
                    dve.tensor_tensor(k_end[:, :], qkb[:, 1, :], exp_end[:, :], ALU.mult).then_inc(levels_ready, 1)

                def norm_first(t):
                    dve.wait_ge(made["OUT"], t)
                    dve.wait_ge(x_loaded, 16 * t)
                    dve.scalar_tensor_tensor(x_in[:, :], x_in[:, :], ALPHA, place["OUT"][:, :], ALU.mult,
                                             ALU.add).then_inc(read["OUT"], 1)
                    dve.wait_ge(read["OUT"], t + 1)
                    for c in range(2):
                        last = dve.bn_stats(stats[:, c, :], x_in[:, c * 512:(c + 1) * 512])
                    last.then_inc(norm_step, 1)
                    dve.wait_ge(norm_step, 4 * (t - 1) + 1)
                    dve.sem_inc(passed, 1)
                    dve.bn_aggr(moments[:, :], stats[:, :, :].rearrange("p c s -> p (c s)")).then_inc(var_ready, 1)

                def norm_second(t):
                    at = 4 * (t - 1) + 1
                    dve.wait_ge(root_ready, t)
                    dve.reciprocal(lstd[:, 1:2], lstd[:, 0:1]).then_inc(norm_step, 1)
                    dve.wait_ge(norm_step, at + 1)
                    dve.tensor_scalar(x_in[:, :], x_in[:, :], moments[:, 0:1], lstd[:, 1:2], ALU.subtract,
                                      ALU.mult).then_inc(norm_step, 1)
                    dve.wait_ge(norm_step, at + 2)
                    dve.tensor_tensor(x_in[:, :], x_in[:, :], ln[:, 0, :], ALU.mult).then_inc(norm_step, 1)
                    dve.wait_ge(norm_step, at + 3)
                    dve.tensor_tensor(x_in[:, :], x_in[:, :], ln[:, 1, :], ALU.add).then_inc(h1_ready, 1)

                def body(t, s):
                    done = [0]

                    def link(ins):
                        done[0] += 1
                        ins.then_inc(dve_step, 1)
                        dve.wait_ge(dve_step, MIX_STEPS * t + done[0])

                    def heads(x, w):
                        return x.rearrange("p (h w) -> p h w", w=w)

                    def each(kind, width, rows=slice(0, P), hs=slice(0, HEADS_SSD)):
                        n = rows.stop - rows.start
                        return scal[rows, s, kind, hs].unsqueeze(2).to_broadcast([n, hs.stop - hs.start, width])

                    dve.tensor_copy(scal[:, s, :, :], scalars[:, bass.ds(t, 1), :, :].rearrange("p t k h -> p (t k) h")
                                    ).then_inc(scal_ready, 1)
                    dve.wait_ge(scal_ready, t + 1)
                    dve.wait_ge(read["X"], t + 1)
                    if not first(t):
                        dve.wait_ge(made["HN"], t)
                    dve.tensor_tensor(heads(xdt[:, :], 64), heads(xs[:, :], 64), each(1, 64), ALU.mult)
                    dve.tensor_tensor(heads(xend[:, :], 64), heads(xs[:, :], 64), each(4, 64), ALU.mult)
                    for h in range(GLA_BLOCKS):
                        dve.wait_ge(made[f"L{h}"], t + 1)
                        dve.tensor_tensor(masked[:, :], place[f"L{h}"][:, :],
                                          level_mask[:, :, :].rearrange("p l u -> p (l u)"),
                                          ALU.mult).then_inc(read[f"L{h}"], 1)
                        dve.wait_ge(read[f"L{h}"], t + 1)
                        dve.tensor_reduce(att[:, h, :], masked[:, :].rearrange("p (l u) -> p u l", u=P),
                                          AX, ALU.add).then_inc(att_ready, 1)
                        dve.wait_ge(att_ready, GLA_BLOCKS * t + h + 1)
                    dve.tensor_tensor(heads(skip[:, :], 64), heads(xs[:, :], 64),
                                      d_row[:, :].unsqueeze(2).to_broadcast([P, HEADS_SSD, 64]),
                                      ALU.mult).then_inc(skip_ready, 1)
                    for g in range(2):
                        dve.wait_ge(read[f"CS{g}"], t + 1)
                        part = decay[:, 8 * g:8 * g + 8, :]
                        last = dve.tensor_tensor(part, part, place["CB"][:, g * 512:g * 512 + P].unsqueeze(1)
                                                 .to_broadcast([P, 8, P]), ALU.mult)
                    last.then_inc(decay_ready, 1)
                    if not first(t):
                        norm_first(t)
                    if not final(t):
                        exponents(t + 1)
                    if not first(t):
                        norm_second(t)
                    dve.wait_ge(o_root, t + 1)
                    link(dve.reciprocal(ms[:, 2, 0:4], ms[:, 1, 0:4]))
                    dve.wait_ge(gate_loaded, 32 * (t + 1))
                    for h in range(GLA_BLOCKS):
                        e = slice(h * 256, (h + 1) * 256)
                        last = dve.scalar_tensor_tensor(o_sb[:, e], place["O"][:, e], ms[:, 2, h:h + 1],
                                                        gate_in[:, 0, e], ALU.mult, ALU.mult)
                    last.then_inc(og_ready, 1)
                    dve.wait_ge(og_ready, t + 1)
                    dve.sem_inc(read["O"], 1)
                    dve.wait_ge(made["SN"], t + 1)
                    for h in range(GLA_BLOCKS):
                        e = slice(h * 256, (h + 1) * 256)
                        last = dve.scalar_tensor_tensor(state[:, e], state[:, e], b_last[:, s, h:h + 1],
                                                        place["SN"][:, e], ALU.mult, ALU.add)
                    last.then_inc(state_ready, 1)
                    dve.wait_ge(state_ready, t + 1)
                    dve.sem_inc(read["SN"], 1)
                    if not final(t):
                        level_operands(t + 1)
                    dve.wait_ge(made["YO"], t + 1)
                    dve.tensor_tensor(heads(y_sb[:, :], 64), heads(place["YO"][:, :], 64), each(3, 64),
                                      ALU.mult).then_inc(read["YO"], 1)
                    dve.wait_ge(read["YO"], t + 1)
                    dve.tensor_tensor(y_sb[:, :], y_sb[:, :], place["YD"][:, :], ALU.add).then_inc(read["YD"], 1)
                    dve.wait_ge(read["YD"], t + 1)
                    dve.tensor_tensor(y_sb[:, :], y_sb[:, :], gate_in[:, 1, :], ALU.mult).then_inc(y_gated, 1)
                    dve.wait_ge(made["HN"], t + 1)
                    sides = [slice(64 * g, 64 * g + 64) for g in range(2)]
                    for g, rows in enumerate(sides):
                        last = dve.tensor_tensor(heads(hstate[rows, :], 64), heads(hstate[rows, :], 64),
                                                 each(5, 64, rows, slice(8 * g, 8 * g + 8)), ALU.mult)
                    link(last)
                    for g, rows in enumerate(sides):
                        last = dve.tensor_tensor(hstate[rows, :], hstate[rows, :],
                                                 place["HN"][rows, g * 512:(g + 1) * 512], ALU.add)
                    last.then_inc(hstate_ready, 1)
                    dve.wait_ge(hstate_ready, t + 1)
                    dve.sem_inc(read["HN"], 1)
                    dve.wait_ge(y_root, t + 1)
                    link(dve.reciprocal(ms[:, 2, 4:6], ms[:, 1, 4:6]))
                    for g in range(2):
                        e = slice(g * 512, (g + 1) * 512)
                        last = dve.tensor_scalar(y_sb[:, e], y_sb[:, e], ms[:, 2, 4 + g:5 + g], None, ALU.mult)
                    last.then_inc(yg_ready, 1)
                    assert done[0] == MIX_STEPS

                exponents(0)
                level_operands(0)
                tiles(dve, body)
                norm_first(TILES)
                norm_second(TILES)


def build_memory_tables(nc, memT, wk, wqT, wv, wo, mem_scores_w, mem_values_w):
    with ExitStack() as ctx:
        sb, psum, sem = allocators(nc, ctx)
        mem_sb = sb("mem_sb", [P, KC, MEM], F32)
        weights = [sb(f"mem_weight{i}", [P, KC, D], F32) for i in range(2)]
        keysT = sb("keysT", [P, KC, MEM], F32)
        valuesT = sb("valuesT", [P, KC, MEM], F32)
        groups = [psum(f"mem_group{i}", [P, D], F32) for i in range(4)]
        mem_loaded = sem("mem_loaded")
        weight_loaded = [sem(f"mem_weight_loaded{i}") for i in range(2)]
        group_done = sem("mem_group_done")
        group_copied = sem("mem_group_copied")
        CB = KC // HEADS_CA
        GROUP_BLOCKS = D // MEM
        N_PROJ = KC // GROUP_BLOCKS

        def destination(g):
            if g < 2 * N_PROJ:
                t = keysT if g < N_PROJ else valuesT
                b = (g % N_PROJ) * GROUP_BLOCKS
                return t[:, b:b + GROUP_BLOCKS, :].rearrange("p b m -> p (b m)")
            t = mem_scores_w if g < 2 * N_PROJ + KC else mem_values_w
            return t[:, (g - 2 * N_PROJ) % KC, :]

        with nc.Block() as block:
            @block.sync
            def _(sp):
                sp.dma_start(mem_sb[:, :, :], memT).then_inc(mem_loaded, 16)
                sp.dma_start(weights[0][:, :, :], wk).then_inc(weight_loaded[0], 16)
                sp.dma_start(weights[1][:, :, :], wv).then_inc(weight_loaded[1], 16)
                sp.wait_ge(group_done, N_PROJ)
                sp.dma_start(weights[0][:, :, :], wqT).then_inc(weight_loaded[0], 16)
                sp.wait_ge(group_done, 2 * N_PROJ)
                sp.dma_start(weights[1][:, :, :], wo).then_inc(weight_loaded[1], 16)

            @block.tensor
            def _(pe):
                pe.wait_ge(mem_loaded, 16)
                for g in range(2 * N_PROJ):
                    if g % N_PROJ == 0:
                        pe.wait_ge(weight_loaded[g // N_PROJ], 16)
                    for b in range(GROUP_BLOCKS):
                        c = (g % N_PROJ) * GROUP_BLOCKS + b
                        for k in range(KC):
                            last = pe.matmul(groups[g % 4][:, b * MEM:(b + 1) * MEM],
                                             weights[g // N_PROJ][:, k, c * P:(c + 1) * P], mem_sb[:, k, :],
                                             start=(k == 0), stop=(k == KC - 1))
                    last.then_inc(group_done, 1)
                for g in range(2 * N_PROJ, 2 * N_PROJ + 2 * KC):
                    pe.wait_ge(group_copied, g - 3)
                    r = (g - 2 * N_PROJ) % KC
                    if g < 2 * N_PROJ + KC:
                        if r == 0:
                            pe.wait_ge(group_copied, N_PROJ)
                            pe.wait_ge(weight_loaded[0], 32)
                        for h in range(HEADS_CA):
                            for c in range(CB):
                                last = pe.matmul(groups[g % 4][:, h * MEM:(h + 1) * MEM],
                                                 weights[0][:, CB * h + c, r * P:(r + 1) * P],
                                                 keysT[:, CB * h + c, :], start=(c == 0), stop=(c == CB - 1))
                    else:
                        if r == 0:
                            pe.wait_ge(group_copied, 2 * N_PROJ)
                            pe.wait_ge(weight_loaded[1], 32)
                        h, mb = r // 2, r % 2
                        for n in range(2):
                            for c in range(CB):
                                last = pe.matmul(groups[g % 4][:, n * 512:(n + 1) * 512],
                                                 valuesT[:, CB * h + c, mb * P:(mb + 1) * P],
                                                 weights[1][:, CB * h + c, n * 512:(n + 1) * 512],
                                                 start=(c == 0), stop=(c == CB - 1))
                    last.then_inc(group_done, 1)

            @block.scalar
            def _(act):
                for g in range(2 * N_PROJ + 2 * KC):
                    act.wait_ge(group_done, g + 1)
                    act.activation(destination(g), groups[g % 4][:, :], ACT.Copy).then_inc(group_copied, 1)


def attend_and_retrieve(nc, h1_dram, peer_wq, peer_keysT, peer_u, peer_v, ln_rows, ident_dram, iota_dram, out,
                        mem_scores_w, mem_values_w):
    with ExitStack() as ctx:
        sb, psum, sem = allocators(nc, ctx)
        pwq = sb("pwq", [P, KC, D], F32)
        keys = sb("keys", [P, NKEYS], F32)
        ident = sb("ident3", [P, P], F32)
        iota16 = sb("iota16", [P, TOPK], F32)
        eps = sb("eps3", [P, 1], F32)
        ln = sb("ln_rows3", [P, 4, D], F32)
        h1 = sb("h1_tile", [P, D], F32)
        h2 = sb("h2", [P, 2, D], F32)
        hT = sb("hT3", [P, KC, P], F32)
        pqT = sb("pqT", [P, PHEADS, P], F32)
        work = sb("work3", [P, 4 * D], F32)
        probs = work[:, 0:D]
        probsT = work[:, D:2 * D]
        pre2 = work[:, 2 * D:3 * D]
        scores = work[:, 0:2 * D]
        scores_cut = work[:, 2 * D:4 * D]
        y3 = sb("y3", [P, D], F32)
        u_ring = sb("u_ring", [P, RING, D], F32)
        v_ring = sb("v_ring", [P, RING, D], F32)
        diag = sb("diag", [P, RING, P], F32)
        idx = sb("idx", [P, 2, PICKS], mybir.dt.int32)
        gates = sb("gates", [P, 2, PICKS], F32)
        act_u = sb("act_u", [P, 2, TOPK], F32)
        gelu_u = sb("gelu_u", [P, 2, TOPK], F32)
        w_v = sb("w_v", [P, 2, TOPK], F32)
        vals = sb("vals", [P, 2 * PHEADS, TOPK], F32)
        vidx = sb("vidx", [P, 2 * PHEADS, TOPK], U32)
        vidx_f = sb("vidx_f", [P, 2 * PHEADS, TOPK], F32)
        best = sb("best", [P, PHEADS, TOPK], F32)
        bidx = sb("bidx", [P, PHEADS, TOPK], U32)
        bhalf = sb("bhalf", [P, 2, PICKS], U32)
        bhalf_f = sb("bhalf_f", [P, 2, PICKS], F32)
        ihalf = sb("ihalf", [P, 2, PICKS], F32)
        gexp = sb("gexp", [P, PHEADS, TOPK], F32)
        gsum = sb("gsum", [P, PHEADS], F32)
        ginv = sb("ginv", [P, PHEADS], F32)
        negmax = sb("negmax", [P, HEADS_CA], F32)
        rowmax = sb("rowmax", [P, HEADS_CA], F32)
        psums = sb("prob_sums", [P, HEADS_CA], F32)
        pinv = sb("prob_inv", [P, HEADS_CA], F32)
        stats = sb("stats3", [P, 2, 2, 6], F32)
        moments = sb("moments3", [P, 2, 2], F32)
        std = sb("std3", [P, 2], F32)
        rstd = sb("rstd3", [P, 2], F32)

        acc = psum("acc", [P, D], F32)
        small = psum("small3", [P, D], F32)
        wide = psum("wide3", [P, 2 * D], F32)

        consts_loaded = sem("consts3_loaded")
        pwq_loaded = sem("pwq_loaded")
        eps_ready = sem("eps3_ready")
        h1_loaded = sem("h1_loaded")
        u_landed = [sem(f"u_landed{i}") for i in range(RING)]
        v_landed = [sem(f"v_landed{i}") for i in range(RING)]
        dot_done = sem("dot_done")
        gelu_done = sem("gelu_done")
        w_ready = sem("w_ready")
        diag_ready = sem("diag_ready")
        v_used = sem("v_used")
        acc_copied = sem("acc_copied")
        y3_ready = sem("y3_ready")
        y3_stored, y3_free = sem("y3_stored"), sem("y3_free")
        var3_ready, std3_ready = sem("var3_ready"), sem("std3_ready")
        h1T_made, h1T_ready = sem("h1T_made"), sem("h1T_ready")
        att_made = sem("att_made")
        negmax_ready = sem("negmax_ready")
        probs_exp = sem("probs_exp")
        probs_ready = sem("probs_ready")
        probsT_made, probsT_ready = sem("probsT_made"), sem("probsT_ready")
        ca_made = sem("ca_made")
        var2_ready, std2_ready = sem("var2_ready"), sem("std2_ready")
        h2_ready = sem("h2_ready")
        h2T_made, h2T_ready = sem("h2T_made"), sem("h2T_ready")
        pq_made, pq_ready = sem("pq_made"), sem("pq_ready")
        keyscores_made, keyscores_ready = sem("keyscores_made"), sem("keyscores_ready")
        gate_logits, gate_exp = sem("gate_logits"), sem("gate_exp")
        idx_ready = sem("idx_ready")
        front_step = sem("front_step")
        tail_step = sem("tail_step")
        waits_passed = [sem("pool_waits_passed"), sem("dve_waits_passed")]

        def tiles(engine, body, last):
            body(0, 0, True)
            with engine.Fori(0, (TILES - 2) // 2) as i:
                body(2 * i + 1, 1, True)
                body(2 * i + 2, 0, True)
            body(TILES - 1, 1, False)
            last(TILES, 0)

        def lagged(t, s, n):
            return (t, s, n - LAG) if n >= LAG else (t - 1, 1 - s, PICKS + n - LAG)

        with nc.Block() as block:
            @block.sync
            def _(sp):
                sp.dma_start(ident[:, :], ident_dram).then_inc(consts_loaded, 16)
                sp.dma_start(iota16[:, :], iota_dram).then_inc(consts_loaded, 16)
                sp.dma_start(ln[:, :, :], ln_rows).then_inc(consts_loaded, 16)
                sp.dma_start(keys[:, :], peer_keysT).then_inc(consts_loaded, 16)
                sp.dma_start(h1[:, :], h1_dram[0]).then_inc(h1_loaded, 16)
                sp.dma_start(pwq[:, :, :], peer_wq).then_inc(pwq_loaded, 16)
                sp.sem_inc(y3_free, 1)

                def next_h1(t):
                    sp.wait_ge(h2_ready, t)
                    sp.dma_start(h1[:, :], h1_dram[t]).then_inc(h1_loaded, 16)

                def store_y3(t):
                    sp.wait_ge(y3_ready, t)
                    sp.dma_start(out[t - 1], y3[:, :]).then_inc(y3_stored, 16)
                    sp.wait_ge(y3_stored, 16 * t)
                    sp.sem_inc(y3_free, 1)

                next_h1(1)
                with sp.Fori(1, TILES - 1) as t:
                    next_h1(t + 1)
                    store_y3(t)
                store_y3(TILES - 1)
                sp.wait_ge(y3_ready, TILES)
                sp.dma_start(out[TILES - 1], y3[:, :]).then_inc(y3_stored, 16)
                sp.wait_ge(y3_stored, 16 * TILES)

            @block.gpsimd
            def _(pool):
                def gather(ring, landed, table, s, n):
                    pool.indirect_dma_start(out=ring[:, n % RING, :], out_offset=None, in_=table,
                                            in_offset=bass.IndirectOffsetOnAxis(ap=idx[:, s, n:n + 1], axis=0)
                                            ).then_inc(landed[n % RING], 16)

                def gather_u(t, s, n):
                    if n == 0:
                        pool.wait_ge(idx_ready, t + 1)
                    if not (isinstance(t, int) and PICKS * t + n < RING):
                        pool.wait_ge(dot_done, PICKS * t + n - RING + 1)
                        pool.sem_inc(waits_passed[0], 1)
                    gather(u_ring, u_landed, peer_u, s, n)

                def gather_v(t, s, n):
                    if not (isinstance(t, int) and PICKS * t + n < RING):
                        pool.wait_ge(v_used, PICKS * t + n - RING + 1)
                        pool.sem_inc(waits_passed[0], 1)
                    gather(v_ring, v_landed, peer_v, s, n)

                def body(t, s, front):
                    for n in range(PICKS):
                        gather_u(t, s, n)
                        if n >= LAG or not (isinstance(t, int) and t == 0):
                            gather_v(*lagged(t, s, n))

                def last(t, s):
                    for n in range(LAG):
                        gather_v(*lagged(t, s, n))

                tiles(pool, body, last)

            @block.tensor
            def _(pe):
                def combine(t, s, n):
                    pe.wait_ge(diag_ready, PICKS * t + n + 1)
                    pe.wait_ge(v_landed[n % RING], 16 * (PICKS // RING * t + n // RING + 1))
                    if n == 0 and not (isinstance(t, int) and t == 0):
                        pe.wait_ge(acc_copied, t)
                    for c in range(2):
                        last = pe.matmul(acc[:, c * 512:(c + 1) * 512], diag[:, n % RING, :],
                                         v_ring[:, n % RING, c * 512:(c + 1) * 512],
                                         start=(n == 0), stop=(n == PICKS - 1))
                    last.then_inc(v_used, 1)

                def to_T(source):
                    for k in range(KC):
                        last = pe.transpose(small[:, k * P:(k + 1) * P], source[:, k * P:(k + 1) * P], ident[:, :])
                    return last

                def front(f, s, n):
                    if n == 18:
                        pe.wait_ge(h1_loaded, 16 * (f + 1))
                        if not (isinstance(f, int) and f == 0):
                            pe.wait_ge(pq_ready, f)
                        to_T(h1).then_inc(h1T_made, 1)
                    if 22 <= n < 30:
                        q = n - 22
                        if q == 0:
                            pe.wait_ge(h1T_ready, f + 1)
                            if not (isinstance(f, int) and f == 0):
                                pe.wait_ge(keyscores_ready, f)
                        for k in range(2 * (q % 4), 2 * (q % 4) + 2):
                            c = q // 4
                            last = pe.matmul(wide[:, c * 512:(c + 1) * 512], hT[:, k, :],
                                             mem_scores_w[:, k, c * 512:(c + 1) * 512],
                                             start=(k == 0), stop=(k == KC - 1))
                        if q == 7:
                            last.then_inc(att_made, 1)
                    if n == 40:
                        pe.wait_ge(probs_ready, f + 1)
                        to_T(probs).then_inc(probsT_made, 1)
                    if 44 <= n < 52:
                        q = n - 44
                        if q == 0:
                            pe.wait_ge(probsT_ready, f + 1)
                        for k in range(2 * (q % 4), 2 * (q % 4) + 2):
                            c = q // 4
                            last = pe.matmul(wide[:, D + c * 512:D + (c + 1) * 512],
                                             probsT[:, k * P:(k + 1) * P],
                                             mem_values_w[:, k, c * 512:(c + 1) * 512],
                                             start=(k == 0), stop=(k == KC - 1))
                        if q == 7:
                            last.then_inc(ca_made, 1)
                    if n == 62:
                        pe.wait_ge(h2_ready, f + 1)
                        to_T(h2[:, s, :]).then_inc(h2T_made, 1)
                    if 66 <= n < 82:
                        q = n - 66
                        if q == 0:
                            pe.wait_ge(h2T_ready, f + 1)
                            pe.wait_ge(pwq_loaded, 16)
                        for k in range(4 * (q % 2), 4 * (q % 2) + 4):
                            h = q // 2
                            last = pe.matmul(small[:, h * P:(h + 1) * P], pwq[:, k, h * P:(h + 1) * P],
                                             hT[:, k, :], start=(k == 0), stop=(k == KC - 1))
                        if q == 15:
                            last.then_inc(pq_made, 1)
                    if 86 <= n < 90:
                        q = n - 86
                        if q == 0:
                            pe.wait_ge(pq_ready, f + 1)
                        for r in range(4 * q, 4 * q + 4):
                            half, h = r // PHEADS, r % PHEADS
                            last = pe.matmul(wide[:, r * NKEYS:(r + 1) * NKEYS],
                                             pqT[64 * half:64 * half + 64, h, :],
                                             keys[64 * half:64 * half + 64, :], start=True, stop=True)
                        if q == 3:
                            last.then_inc(keyscores_made, 1)

                pe.wait_ge(consts_loaded, 64)
                for n in range(PICKS):
                    front(0, 0, n)

                def body(t, s, next_front):
                    for n in range(PICKS):
                        if n >= LAG or not (isinstance(t, int) and t == 0):
                            combine(*lagged(t, s, n))
                        if next_front:
                            front(t + 1, 1 - s, n)

                def last(t, s):
                    for n in range(LAG):
                        combine(*lagged(t, s, n))

                tiles(pe, body, last)

            @block.scalar
            def _(act):
                def gelus(t, h):
                    act.wait_ge(dot_done, PICKS * t + TOPK * (h + 1))
                    act.activation(gelu_u[:, h % 2, :], act_u[:, h % 2, :], ACT.Gelu).then_inc(gelu_done, 1)

                def spread(t, s, n):
                    h, j = n // TOPK, n % TOPK
                    if j == 0:
                        act.wait_ge(w_ready, PHEADS * t + h + 1)
                    if not (isinstance(t, int) and PICKS * t + n < RING):
                        act.wait_ge(v_used, PICKS * t + n - RING + 1)
                    act.activation(diag[:, n % RING, :], ident[:, :], ACT.Copy,
                                   scale=w_v[:, h % 2, j:j + 1]).then_inc(diag_ready, 1)

                def front(f, s, n):
                    if n == 20:
                        act.wait_ge(h1T_made, f + 1)
                        act.activation(hT[:, :, :].rearrange("p k t -> p (k t)"), small[:, :],
                                       ACT.Copy).then_inc(h1T_ready, 1)
                    if n == 34:
                        act.wait_ge(negmax_ready, f + 1)
                        for h in range(HEADS_CA):
                            last = act.activation(probs[:, h * MEM:(h + 1) * MEM], wide[:, h * MEM:(h + 1) * MEM],
                                                  ACT.Exp, bias=negmax[:, h:h + 1], scale=MEM_SCALE,
                                                  accum_out=psums[:, h:h + 1])
                        last.then_inc(probs_exp, 1)
                    if n == 42:
                        act.wait_ge(probsT_made, f + 1)
                        act.activation(probsT, small[:, :], ACT.Copy).then_inc(probsT_ready, 1)
                    if n == 57:
                        act.wait_ge(var2_ready, f + 1)
                        act.activation(std[:, 0:1], moments[:, 0, 1:2], ACT.Sqrt,
                                       bias=eps[:, :]).then_inc(std2_ready, 1)
                    if n == 64:
                        act.wait_ge(h2T_made, f + 1)
                        act.activation(hT[:, :, :].rearrange("p k t -> p (k t)"), small[:, :],
                                       ACT.Copy).then_inc(h2T_ready, 1)
                    if n == 84:
                        act.wait_ge(pq_made, f + 1)
                        act.activation(pqT[:, :, :].rearrange("p h t -> p (h t)"), small[:, :],
                                       ACT.Copy).then_inc(pq_ready, 1)
                    if n == 91:
                        act.wait_ge(keyscores_made, f + 1)
                        for c in range(2):
                            last = act.activation(scores[:, c * D:(c + 1) * D], wide[:, c * D:(c + 1) * D], ACT.Copy)
                        last.then_inc(keyscores_ready, 1)
                    if n == 118:
                        act.wait_ge(gate_logits, f + 1)
                        act.activation(gexp[:, :, :], gexp[:, :, :], ACT.Exp).then_inc(gate_exp, 1)

                act.wait_ge(consts_loaded, 64)
                act.wait_ge(eps_ready, 1)
                for n in range(PICKS):
                    front(0, 0, n)

                def norm3(t):
                    act.wait_ge(var3_ready, t)
                    act.activation(std[:, 1:2], moments[:, 1, 1:2], ACT.Sqrt, bias=eps[:, :]).then_inc(std3_ready, 1)

                def body(t, s, next_front):
                    for n in range(PICKS):
                        if n % TOPK == 0 and n > 0:
                            gelus(t, n // TOPK - 1)
                        elif n == 0 and not (isinstance(t, int) and t == 0):
                            gelus(t - 1, PHEADS - 1)
                        if n >= LAG or not (isinstance(t, int) and t == 0):
                            spread(*lagged(t, s, n))
                        if n == LAG + 1 and not (isinstance(t, int) and t == 0):
                            norm3(t)
                        if next_front:
                            front(t + 1, 1 - s, n)

                def last(t, s):
                    gelus(t - 1, PHEADS - 1)
                    for n in range(LAG):
                        spread(*lagged(t, s, n))
                    norm3(t)

                tiles(act, body, last)

            @block.vector
            def _(dve):
                def dot(t, s, n):
                    dve.wait_ge(u_landed[n % RING], 16 * (PICKS // RING * t + n // RING + 1))
                    row = u_ring[:, n % RING, :]
                    dve.tensor_tensor_reduce(out=row, in0=row, in1=h2[:, s, :], scale=1.0, scalar=0.0,
                                             op0=ALU.mult, op1=ALU.add,
                                             accum_out=act_u[:, (n // TOPK) % 2, n % TOPK:n % TOPK + 1]
                                             ).then_inc(dot_done, 1)

                def weigh(t, s, h):
                    dve.wait_ge(gelu_done, PHEADS * t + h + 1)
                    if not (isinstance(t, int) and PHEADS * t + h < 2):
                        dve.wait_ge(diag_ready, PICKS * t + TOPK * (h - 1))
                    dve.tensor_tensor(w_v[:, h % 2, :], gelu_u[:, h % 2, :], gates[:, s, h * TOPK:(h + 1) * TOPK],
                                      ALU.mult).then_inc(w_ready, 1)

                def norm_stats(x, which, step, at):
                    for c in range(2):
                        last = dve.bn_stats(stats[:, which, c, :], x[:, c * 512:(c + 1) * 512])
                    last.then_inc(step, 1)
                    dve.wait_ge(step, at)
                    dve.sem_inc(waits_passed[1], 1)
                    return dve.bn_aggr(moments[:, which, :], stats[:, which, :, :].rearrange("p c s -> p (c s)"))

                def norm_apply(to, x, which, step, at):
                    dve.reciprocal(rstd[:, which:which + 1], std[:, which:which + 1]).then_inc(step, 1)
                    dve.wait_ge(step, at)
                    dve.tensor_scalar(x, x, moments[:, which, 0:1], rstd[:, which:which + 1],
                                      ALU.subtract, ALU.mult).then_inc(step, 1)
                    dve.wait_ge(step, at + 1)
                    dve.tensor_tensor(x, x, ln[:, 2 * which, :], ALU.mult).then_inc(step, 1)
                    dve.wait_ge(step, at + 2)
                    return dve.tensor_tensor(to, x, ln[:, 2 * which + 1, :], ALU.add)

                def norm3_first(t):
                    at = TAIL_STEPS * (t - 1)
                    dve.wait_ge(v_used, PICKS * t)
                    dve.wait_ge(y3_free, t)
                    return at

                def norm3_a(t, s):
                    at = norm3_first(t)
                    dve.scalar_tensor_tensor(y3[:, :], h2[:, s, :], ALPHA, acc[:, :], ALU.mult,
                                             ALU.add).then_inc(acc_copied, 1)
                    dve.wait_ge(acc_copied, t)
                    norm_stats(y3[:, :], 1, tail_step, at + 1).then_inc(var3_ready, 1)

                def norm3_b(t):
                    at = TAIL_STEPS * (t - 1)
                    dve.wait_ge(std3_ready, t)
                    norm_apply(y3[:, :], y3[:, :], 1, tail_step, at + 2).then_inc(y3_ready, 1)

                def front(f, s, n):
                    at = FRONT_STEPS * f

                    def link(ins, k):
                        ins.then_inc(front_step, 1)
                        dve.wait_ge(front_step, at + k)
                        dve.sem_inc(waits_passed[1], 1)

                    if n == 32:
                        dve.wait_ge(att_made, f + 1)
                        link(dve.tensor_reduce(rowmax[:, :], wide[:, 0:D].rearrange("p (h m) -> p h m", m=MEM),
                                               AX, ALU.max), 1)
                        dve.tensor_scalar(negmax[:, :], rowmax[:, :], -MEM_SCALE, None,
                                          ALU.mult).then_inc(negmax_ready, 1)
                    if n == 37:
                        dve.wait_ge(probs_exp, f + 1)
                        link(dve.reciprocal(pinv[:, :], psums[:, :]), 2)
                        p4 = probs.rearrange("p (h m) -> p h m", m=MEM)
                        dve.tensor_tensor(p4, p4, pinv[:, :].unsqueeze(2).to_broadcast([P, HEADS_CA, MEM]),
                                          ALU.mult).then_inc(probs_ready, 1)
                    if n == 54:
                        dve.wait_ge(ca_made, f + 1)
                        link(dve.scalar_tensor_tensor(pre2, h1[:, :], ALPHA, wide[:, D:2 * D], ALU.mult,
                                                      ALU.add), 3)
                        norm_stats(pre2, 0, front_step, at + 4).then_inc(var2_ready, 1)
                    if n == 59:
                        dve.wait_ge(std2_ready, f + 1)
                        norm_apply(h2[:, s, :], pre2, 0, front_step, at + 5).then_inc(h2_ready, 1)
                    rows = range(2 * PHEADS)
                    if n == 93:
                        dve.wait_ge(keyscores_ready, f + 1)
                        dve.wait_ge(h2_ready, f + 1)
                        dve.sem_inc(waits_passed[1], 1)
                        for r in rows:
                            last = dve.max(vals[:, r, 0:8], scores[:, r * NKEYS:(r + 1) * NKEYS])
                        link(last, 8)
                    if n == 95:
                        for r in rows:
                            dve.max_index(vidx[:, r, 0:8], vals[:, r, 0:8], scores[:, r * NKEYS:(r + 1) * NKEYS])
                    if n == 97:
                        for r in rows:
                            last = dve.match_replace(scores_cut[:, r * NKEYS:(r + 1) * NKEYS], vals[:, r, 0:8],
                                                     scores[:, r * NKEYS:(r + 1) * NKEYS], LEAST)
                        link(last, 9)
                    if n == 99:
                        for r in rows:
                            last = dve.max(vals[:, r, 8:16], scores_cut[:, r * NKEYS:(r + 1) * NKEYS])
                        link(last, 10)
                    if n == 101:
                        for r in rows:
                            dve.max_index(vidx[:, r, 8:16], vals[:, r, 8:16], scores_cut[:, r * NKEYS:(r + 1) * NKEYS])
                        v4 = vals[:, :, :].rearrange("p (c h) k -> p c h k", c=2)
                        link(dve.tensor_tensor(scores.rearrange("p (h i j) -> p h i j", i=TOPK, j=TOPK),
                                               v4[:, 0, :, :].unsqueeze(3).to_broadcast([P, PHEADS, TOPK, TOPK]),
                                               v4[:, 1, :, :].unsqueeze(2).to_broadcast([P, PHEADS, TOPK, TOPK]),
                                               ALU.add), 11)
                    cand = [scores[:, h * 256:(h + 1) * 256] for h in range(PHEADS)]
                    cut = [scores_cut[:, h * 256:(h + 1) * 256] for h in range(PHEADS)]
                    if n == 104:
                        for h in range(PHEADS):
                            last = dve.max(best[:, h, 0:8], cand[h])
                        link(last, 12)
                    if n == 106:
                        for h in range(PHEADS):
                            dve.max_index(bidx[:, h, 0:8], best[:, h, 0:8], cand[h])
                    if n == 108:
                        for h in range(PHEADS):
                            last = dve.match_replace(cut[h], best[:, h, 0:8], cand[h], LEAST)
                        link(last, 13)
                    if n == 110:
                        for h in range(PHEADS):
                            last = dve.max(best[:, h, 8:16], cut[h])
                        link(last, 14)
                    if n == 112:
                        for h in range(PHEADS):
                            last = dve.max_index(bidx[:, h, 8:16], best[:, h, 8:16], cut[h])
                        link(last, 15)
                        flat = bidx[:, :, :].rearrange("p h k -> p (h k)")
                        dve.tensor_scalar(bhalf[:, 0, :], flat, 4, None, ALU.logical_shift_right)
                        dve.tensor_scalar(bhalf[:, 1, :], flat, 15, None, ALU.bitwise_and)
                        dve.tensor_copy(vidx_f[:, :, :], vidx[:, :, :])
                        dve.tensor_tensor(gexp[:, :, :], best[:, :, :],
                                          best[:, :, 0:1].to_broadcast([P, PHEADS, TOPK]),
                                          ALU.subtract).then_inc(gate_logits, 1)
                        dve.wait_ge(gate_logits, f + 1)
                        link(dve.tensor_copy(bhalf_f[:, :, :], bhalf[:, :, :]), 16)
                    four = "p (h k j) -> p h k j"
                    for half, (where, n0) in enumerate(((scores_cut, 114), (scores, 116))):
                        if n == n0:
                            w4 = where.rearrange(four, k=TOPK, j=TOPK)
                            w3 = where.rearrange("p (a j) -> p a j", j=TOPK)
                            link(dve.tensor_tensor(w3, bhalf_f[:, half, :].unsqueeze(2).to_broadcast([P, PICKS, TOPK]),
                                                   iota16[:, :].unsqueeze(1).to_broadcast([P, PICKS, TOPK]),
                                                   ALU.is_equal), 17 + 3 * half)
                            names = vidx_f[:, half * PHEADS:(half + 1) * PHEADS, :]
                            link(dve.tensor_tensor(w4, w4, names.unsqueeze(2).to_broadcast([P, PHEADS, TOPK, TOPK]),
                                                   ALU.mult), 18 + 3 * half)
                            link(dve.tensor_reduce(ihalf[:, half, :], w3, AX, ALU.add), 19 + 3 * half)
                    if n == 118:
                        dve.scalar_tensor_tensor(idx[:, s, :], ihalf[:, 0, :], float(NKEYS), ihalf[:, 1, :],
                                                 ALU.mult, ALU.add).then_inc(idx_ready, 1)
                    if n == 120:
                        dve.wait_ge(gate_exp, f + 1)
                        link(dve.tensor_reduce(gsum[:, :], gexp[:, :, :], AX, ALU.add), 23)
                        link(dve.reciprocal(ginv[:, :], gsum[:, :]), 24)
                        link(dve.tensor_tensor(gates[:, s, :].rearrange("p (h k) -> p h k", k=TOPK), gexp[:, :, :],
                                               ginv[:, :].unsqueeze(2).to_broadcast([P, PHEADS, TOPK]),
                                               ALU.mult), 25)

                dve.memset(eps[:, :], LN_EPS).then_inc(eps_ready, 1)
                dve.wait_ge(consts_loaded, 64)
                for n in range(PICKS):
                    front(0, 0, n)

                def body(t, s, next_front):
                    for n in range(PICKS):
                        dot(t, s, n)
                        if n % TOPK == 2 and n > TOPK:
                            weigh(t, s, n // TOPK - 1)
                        elif n == 2 and not (isinstance(t, int) and t == 0):
                            weigh(t - 1, 1 - s, PHEADS - 1)
                        if n == LAG and not (isinstance(t, int) and t == 0):
                            norm3_a(t, 1 - s)
                        if n == LAG + 4 and not (isinstance(t, int) and t == 0):
                            norm3_b(t)
                        if next_front:
                            front(t + 1, 1 - s, n)

                def last(t, s):
                    weigh(t - 1, 1 - s, PHEADS - 1)
                    norm3_a(t, 1 - s)
                    norm3_b(t)

                tiles(dve, body, last)


def program(nc, a, out):
    scanT = nc.dram_tensor("scanT_dram", (2 * GLA_BLOCKS + XBC_BLOCKS + GLA_BLOCKS, P, SEQ), F32).ap()
    nat = nc.dram_tensor("nat_dram", (3, TILES, P, D), F32).ap()
    h1 = nc.dram_tensor("h1_dram", (TILES, P, D), F32).ap()
    with ExitStack() as ctx:
        sb, psum, sem = allocators(nc, ctx)
        scalars = sb("scalars", [P, TILES, KINDS, HEADS_SSD], F32)
        project_inputs(nc, a, scanT, nat, scalars)
        mix_tokens(nc, a, scanT, nat, scalars, h1)
    with ExitStack() as ctx:
        sb, psum, sem = allocators(nc, ctx)
        mem_scores_w = sb("mem_scores_w", [P, KC, D], F32)
        mem_values_w = sb("mem_values_w", [P, KC, D], F32)
        build_memory_tables(nc, a["memT"], a["wk"], a["wqT"], a["wv"], a["wo"], mem_scores_w, mem_values_w)
        attend_and_retrieve(nc, h1, a["peer_wq"], a["keysT"], a["u"], a["v"], a["ln"], a["ident"], a["iota"],
                            out, mem_scores_w, mem_values_w)


def kernel(**inputs):
    import numpy as np
    import concourse.bacc as _bacc
    from concourse import mybir as _mybir
    from concourse.bass_utils import run_bass_kernel_spmd as _run

    x = {k: np.asarray(v) for k, v in inputs.items()}

    def chunks(w):
        return w.reshape(-1, P, w.shape[-1]).transpose(1, 0, 2)

    def rows(*v):
        return np.broadcast_to(np.stack(v)[None], (P, len(v), v[0].shape[-1]))

    def columns(v):
        return v.reshape(-1, P).T

    w_in = x["w_in"][0]
    q0, k0, v0, r0, g0, z0, c0, t0 = 0, 512, 1024, 2048, 3072, 3088, 4112, 5392
    w_tr = np.concatenate([w_in[:, q0:v0], w_in[:, c0:t0]], 1)
    w_nat = np.concatenate([w_in[:, v0:g0], w_in[:, z0:c0]], 1)
    u = np.arange(P)
    masks = [((u[None] >> lv) % 2 == 1) & ((u[:, None] >> lv) == (u[None] >> lv) - 1) for lv in range(LEVELS)]
    masks.append(u[:, None] == u[None])
    import ml_dtypes
    given = {
        "x": x["x"].reshape(TILES, P, D),
        "xT": chunks(x["x"][0].T),
        "w_low": np.stack([chunks(w_in[:, g0:g0 + RANK]), chunks(w_in[:, t0:t0 + RANK])], 2),
        "w_tr": np.stack([chunks(w_tr[:, i:i + P]) for i in range(0, w_tr.shape[1], P)]),
        "w_nat": np.stack([chunks(w_nat[:, i:i + 512]) for i in range(0, w_nat.shape[1], 512)]),
        "wg2": x["gla_wg2"][0],
        "small_cols": np.concatenate([columns(x["gla_bg"][0]),
                                      x["ssd_conv_w"][0].T.reshape(XBC_BLOCKS, P, CONV).transpose(1, 0, 2)
                                      .reshape(P, -1), columns(x["ssd_conv_b"][0])], 1),
        "small_rows": rows(x["ssd_dt_bias"][0], x["ssd_a_log"][0]),
        "tri": (u[:, None] <= u[None]).astype(np.float32),
        "ident16": np.eye(P, dtype=ml_dtypes.bfloat16),
        "future16": np.where(u[:, None] > u[None], -1e30, 0.0).astype(ml_dtypes.bfloat16),
        "level_mask": np.stack(masks, 1).astype(ml_dtypes.bfloat16),
        "gainT": columns(np.concatenate([np.tile(x["gla_norm_g"][0], GLA_BLOCKS), x["ssd_norm_g"][0]])),
        "d_row": np.broadcast_to(x["ssd_d"][0], (P, HEADS_SSD)),
        "ln1": rows(x["ln1_g"][0], x["ln1_b"][0]),
        "w_out": chunks(x["w_out"][0]),
        "memT": chunks(x["mem"][0].T),
        "wk": chunks(x["ca_wk"][0]), "wqT": chunks(x["ca_wq"][0].T), "wv": chunks(x["ca_wv"][0]),
        "wo": chunks(x["ca_wo"][0]), "peer_wq": chunks(x["peer_wq"][0]),
        "keysT": x["peer_keys"][0].transpose(0, 2, 1).reshape(P, NKEYS),
        "u": x["peer_u"][0], "v": x["peer_v"][0],
        "ln": rows(x["ln2_g"][0], x["ln2_b"][0], x["ln3_g"][0], x["ln3_b"][0]),
        "ident": np.eye(P, dtype=np.float32),
        "iota": np.broadcast_to(np.arange(TOPK, dtype=np.float32), (P, TOPK)),
    }
    nc = _bacc.Bacc("TRN2", target_bir_lowering=False, num_devices=1)
    arrays, args = {}, {}
    for name, v in given.items():
        v = np.ascontiguousarray(v)
        arrays[f"in_{name}_dram"] = v
        args[name] = nc.dram_tensor(f"in_{name}_dram", v.shape, _mybir.dt.from_np(v.dtype), kind="ExternalInput").ap()
    out = nc.dram_tensor("out_0_dram", (TILES, P, D), F32, kind="ExternalOutput").ap()
    program(nc, args, out)
    r = _run(nc, [arrays], core_ids=[0])
    return r.results[0]["out_0_dram"].reshape(1, SEQ, D)
```

```python
from contextlib import ExitStack
import math

import concourse.bass as bass
from concourse import mybir

F32 = mybir.dt.float32
F32R = mybir.dt.float32r
U32 = mybir.dt.uint32
BF16 = mybir.dt.bfloat16
ALU = mybir.AluOpType
ACT = mybir.ActivationFunctionType
AX = mybir.AxisListType.X

P = 128
SEQ = 1024
D = 1024
TILES = SEQ // P
KC = D // P
MEM = 256
HEADS_CA = 4
MEM_SCALE = (D // HEADS_CA) ** -0.5
PHEADS = 8
NKEYS = 128
TOPK = 16
PICKS = PHEADS * TOPK
LAG = TOPK + 4
RING = 4
ALPHA = 2.0 ** 0.25
LN_EPS = 1e-5
LEAST = -3.0e38
GLA_BLOCKS = 4
GATE_TAU = 16.0
Q_SCALE = P ** -0.5
RANK = 16
HEADS_SSD = 16
XBC_BLOCKS = 10
CONV = 4
KINDS = 6
LEVELS = 7
RMS_EPS = 1e-6
MIX_STEPS = 3
FRONT_STEPS = 25
FIRST_STEPS = 19
FIRST_HEADS = 3
FIRST_LATE = 7
FIRST_TOPK_AT = (5, 10, 15, 19, 22, 24, 26, 28, 30, 32, 34, 36, 37, 38)
TOPK_AT = (93, 95, 97, 99, 101, 104, 106, 108, 110, 112, 114, 116, 118, 120)
TAIL_STEPS = 4


def allocators(nc, ctx):
    def sb(name, shape, dt):
        return ctx.enter_context(nc.sbuf_tensor(name, shape, dt))

    def psum(name, shape, dt):
        return ctx.enter_context(nc.psum_tensor(name, shape, dt))

    def sem(name):
        return ctx.enter_context(nc.semaphore(name))

    return sb, psum, sem


def project_inputs(nc, a, scanT_dram, nat_dram, scalars):
    with ExitStack() as ctx:
        sb, psum, sem = allocators(nc, ctx)
        x_h, x_l = sb("x_high", [P, KC, SEQ], F32R), sb("x_low", [P, KC, SEQ], F32R)
        w_low = sb("w_low", [P, KC, 2, RANK], F32)
        w_tr = [sb(f"w_tr{i}", [P, KC, P], F32) for i in range(2)]
        w_tr_h = [sb(f"w_tr_high{i}", [P, KC, P], F32R) for i in range(2)]
        w_tr_l = [sb(f"w_tr_low{i}", [P, KC, P], F32R) for i in range(2)]
        w_nat = sb("w_nat", [P, KC, 512], F32)
        w_nat_h = [sb(f"w_nat_high{i}", [P, KC, 512], F32R) for i in range(2)]
        w_nat_l = [sb(f"w_nat_low{i}", [P, KC, 512], F32R) for i in range(2)]
        wg2 = sb("wg2", [RANK, GLA_BLOCKS * P], F32)
        small_cols = sb("small_cols", [P, GLA_BLOCKS + 5 * XBC_BLOCKS], F32)
        small_rows = sb("small_rows", [P, 2, HEADS_SSD], F32)
        tri = sb("tri1", [P, P], F32)
        ones = sb("ones1", [P, P], F32)
        early = w_nat[:, :, :].rearrange("p k n -> p (k n)")
        carry = early[:, 0:SEQ]
        low = early[0:RANK, SEQ:2 * SEQ]
        stage = [sb(f"stage{i}", [P, SEQ], F32) for i in range(2)]
        padded = [sb(f"padded{i}", [P, SEQ + CONV - 1], F32) for i in range(2)]
        conv = [sb(f"conv{i}", [P, SEQ], F32) for i in range(2)]
        dt_tmp = sb("dt_tmp", [P, 3, TILES * HEADS_SSD], F32)
        a_neg = sb("a_neg", [P, HEADS_SSD], F32)
        a_all = sb("a_all", [P, TILES * HEADS_SSD], F32)
        group = [psum(f"group{i}", [P, 1024], F32) for i in range(4)]
        low_ps, dt_ps = group[2], group[3]
        x_raw = [early[:, i * SEQ:(i + 1) * SEQ] for i in range(4)] + [t[:, :] for t in stage + conv]

        given = sem("given1")
        x_loaded = [sem(f"x_loaded{i}") for i in range(2)]
        x_split, tr_split, nat_split = sem("x_split"), sem("tr_split"), sem("nat_split")
        tr_loaded = [sem(f"tr_loaded{i}") for i in range(2)]
        nat_loaded = sem("nat_loaded")
        waits_passed = sem("pool1_waits_passed")
        low_ready, dt_made = sem("low_ready"), sem("dt_made")
        gate_made, gate_read = sem("gate_made"), sem("gate_read")
        tr_made, tr_read = sem("tr_made"), sem("tr_read")
        nat_made, nat_read = sem("nat_made"), sem("nat_read")
        staged = sem("staged")
        stored = [sem(f"stored{i}") for i in range(2)]
        conv_done = sem("conv_done")
        consts_made = sem("consts1_made")
        act_step, dve_step = sem("act1_step"), sem("dve1_step")
        dt_biased, dt_logged, a_ready, cs_made = sem("dt_biased"), sem("dt_logged"), sem("a_ready"), sem("cs_made")
        cs_exp_in, cs_exp_out = sem("cs_exp_in"), sem("cs_exp_out")
        gate_min, gate_log, gate_sum = sem("gate_min"), sem("gate_log"), sem("gate_sum")

        NQK = 2 * GLA_BLOCKS
        NTR = NQK + XBC_BLOCKS
        taps = small_cols[:, GLA_BLOCKS:GLA_BLOCKS + CONV * XBC_BLOCKS]
        NG, PAIRS = GLA_BLOCKS, TILES // 2

        with nc.Block() as block:
            @block.sync
            def _(sp):
                sp.dma_start(w_low[:, :, :, :], a["w_low"]).then_inc(given, 16)
                for k in range(KC):
                    sp.dma_start(x_raw[k], a["xT"][:, k, :]).then_inc(x_loaded[k // 4], 16)
                for j in range(2):
                    sp.dma_start(w_tr[j][:, :, :], a["w_tr"][j]).then_inc(tr_loaded[j], 16)
                sp.dma_start(wg2[:, :], a["wg2"]).then_inc(given, 16)
                sp.dma_start(small_cols[:, :], a["small_cols"]).then_inc(given, 16)
                sp.dma_start(small_rows[:, :, :], a["small_rows"]).then_inc(given, 16)
                sp.dma_start(tri[:, :], a["tri"]).then_inc(given, 16)

                def next_tr(i, j):
                    sp.wait_ge(tr_split, 2 * (2 * i + j + 1))
                    sp.dma_start(w_tr[j][:, :, :], a["w_tr"][2 * i + 2 + j]).then_inc(tr_loaded[j], 16)

                def next_nat(n):
                    sp.wait_ge(nat_split, 2 * n)
                    sp.dma_start(w_nat[:, :, :], a["w_nat"][n]).then_inc(nat_loaded, 16)

                def store(dst, src_slot, count):
                    sp.wait_ge(staged, count + 1)
                    sp.dma_start(dst, stage[src_slot][:, :]).then_inc(stored[src_slot], 16)

                for j in range(2):
                    next_tr(0, j)
                for g in range(NG):
                    store(scanT_dram[g], 0, 2 * g)
                    store(scanT_dram[NTR + g], 1, 2 * g + 1)
                    next_tr(1 + g // 2, g % 2)
                sp.wait_ge(gate_sum, NG)
                sp.wait_ge(gate_made, NG)
                sp.dma_start(w_nat[:, :, :], a["w_nat"][0]).then_inc(nat_loaded, 16)
                with sp.Fori(NG // 2, NTR // 2 - 2) as i:
                    for j in range(2):
                        store(scanT_dram[2 * i + j], j, NG + 2 * i + j)
                        next_tr(i + 1, j)
                for b in range(NTR - 4, NTR):
                    store(scanT_dram[b], b % 2, NG + b)

                def pairs(kind, half):
                    for q in range(PAIRS):
                        count = NG + NTR + (2 * kind + half) * PAIRS + q
                        sp.wait_ge(staged, count + 1)
                        for e in range(2):
                            sp.dma_start(nat_dram[kind, 2 * q + e, :, half * 512:(half + 1) * 512],
                                         stage[q % 2][:, e * 512:(e + 1) * 512]).then_inc(stored[q % 2], 16)

                with sp.Fori(0, 2) as kind:
                    for half in range(2):
                        next_nat(2 * kind + half + 1)
                        pairs(kind, half)
                next_nat(5)
                for half in range(2):
                    pairs(2, half)
                for j in range(2):
                    sp.wait_ge(stored[j], 16 * ((NG + NTR) // 2 + 2 * 6 * PAIRS // 2))

            @block.gpsimd
            def _(pool):
                def split_tr(i, j):
                    first = isinstance(i, int) and i == 0
                    pool.wait_ge(tr_loaded[j], 16 * (i + 1))
                    if not first:
                        pool.wait_ge(tr_made, 2 * i + j - 1)
                    pool.sem_inc(waits_passed, 1)
                    pool.tensor_copy(w_tr_h[j][:, :, :], w_tr[j][:, :, :]).then_inc(tr_split, 1)
                    pool.wait_ge(tr_split, 2 * (2 * i + j) + 1)
                    pool.sem_inc(waits_passed, 1)
                    pool.tensor_tensor(w_tr_l[j][:, :, :], w_tr[j][:, :, :], w_tr_h[j][:, :, :].bitcast(F32),
                                       ALU.subtract).then_inc(tr_split, 1)

                def split_nat(kind, half):
                    n = 2 * kind + half
                    pool.wait_ge(nat_loaded, 16 * (n + 1))
                    if not (isinstance(kind, int) and kind == 0):
                        pool.wait_ge(nat_made, PAIRS * (n - 1))
                    pool.sem_inc(waits_passed, 1)
                    pool.tensor_copy(w_nat_h[half][:, :, :], w_nat[:, :, :]).then_inc(nat_split, 1)
                    pool.wait_ge(nat_split, 2 * n + 1)
                    pool.sem_inc(waits_passed, 1)
                    pool.tensor_tensor(w_nat_l[half][:, :, :], w_nat[:, :, :], w_nat_h[half][:, :, :].bitcast(F32),
                                       ALU.subtract).then_inc(nat_split, 1)

                for j in range(2):
                    split_tr(0, j)
                with pool.Fori(1, NTR // 2 - 2) as i:
                    for j in range(2):
                        split_tr(i, j)
                pool.wait_ge(nat_loaded, 16)
                for b in range(NTR - 4, NTR):
                    split_tr(b // 2, b % 2)
                    ks = slice(4 * (b % 2), 4 * (b % 2) + 4)
                    if b < NTR - 2:
                        last = pool.tensor_copy(w_nat_h[0][:, ks, :], w_nat[:, ks, :])
                    else:
                        last = pool.tensor_tensor(w_nat_l[0][:, ks, :], w_nat[:, ks, :],
                                                  w_nat_h[0][:, ks, :].bitcast(F32), ALU.subtract)
                    if b % 2 == 1:
                        last.then_inc(nat_split, 1)
                    if b == NTR - 3:
                        pool.wait_ge(nat_split, 1)
                split_nat(0, 1)
                with pool.Fori(1, 3) as kind:
                    for half in range(2):
                        split_nat(kind, half)

            @block.tensor
            def _(pe):
                pe.wait_ge(given, 80)
                for k in range(KC):
                    if k % 4 == 0:
                        pe.wait_ge(x_loaded[k // 4], 64)
                    for c in range(2):
                        pe.matmul(low_ps[0:RANK, c * 512:(c + 1) * 512], w_low[:, k, 0, :],
                                  x_raw[k][:, c * 512:(c + 1) * 512], start=(k == 0), stop=(k == KC - 1))
                for t in range(TILES):
                    for k in range(KC):
                        last = pe.matmul(dt_ps[:, t * RANK:(t + 1) * RANK], x_raw[k][:, t * P:(t + 1) * P],
                                         w_low[:, k, 1, :], start=(k == 0), stop=(k == KC - 1))
                last.then_inc(dt_made, 1)

                def product(to, stationary, moving):
                    terms = ((0, 0), (0, 1), (1, 0))
                    for k in range(KC):
                        for n, (p, q) in enumerate(terms):
                            last = pe.matmul(to, stationary(p, k), moving(q, k), start=(k == 0 and n == 0),
                                             stop=(k == KC - 1 and n == 2))
                    return last

                def transposed(i, j):
                    pe.wait_ge(tr_split, 2 * (2 * i + j + 1))
                    if not (isinstance(i, int) and i == 0):
                        pe.wait_ge(tr_read, 2 * i + j - 1)
                    for c in range(2):
                        last = product(group[j][:, c * 512:(c + 1) * 512],
                                       lambda p, k: (w_tr_h, w_tr_l)[p][j][:, k, :],
                                       lambda q, k: (x_h, x_l)[q][:, k, c * 512:(c + 1) * 512])
                    last.then_inc(tr_made, 1)

                pe.wait_ge(x_split, 2 * KC)
                for j in range(2):
                    transposed(0, j)
                pe.wait_ge(a_ready, 1)
                pe.wait_ge(consts_made, 4)
                pe.matmul(dt_ps[:, 512:512 + P], tri[:, :], a_all[:, :], start=True, stop=True)
                pe.matmul(dt_ps[:, 512 + P:512 + 2 * P], ones[:, :], a_all[:, :], start=True,
                          stop=True).then_inc(cs_made, 1)
                pe.wait_ge(low_ready, 1)
                for g in range(NG):
                    if g >= 1:
                        transposed((g + 1) // 2, (g + 1) % 2)
                        pe.wait_ge(gate_read, g)
                    for c in range(2):
                        last = pe.matmul(low_ps[:, c * 512:(c + 1) * 512], wg2[:, g * P:(g + 1) * P],
                                         low[:, c * 512:(c + 1) * 512], start=True, stop=True)
                    last.then_inc(gate_made, 1)
                transposed(2, 1)
                with pe.Fori(3, NTR // 2) as i:
                    for j in range(2):
                        transposed(i, j)

                def natural(kind, half):
                    pe.wait_ge(nat_split, 2 * (2 * kind + half + 1))
                    for q in range(PAIRS):
                        count = (2 * kind + half) * PAIRS + q
                        if isinstance(count, int) and count < 2:
                            pe.wait_ge(tr_read, NTR)
                        else:
                            pe.wait_ge(nat_read, count - 1)
                        for e in range(2):
                            t = 2 * q + e
                            last = product(group[q % 2][:, e * 512:(e + 1) * 512],
                                           lambda p, k: (x_h, x_l)[p][:, k, t * P:(t + 1) * P],
                                           lambda p, k: (w_nat_h, w_nat_l)[p][half][:, k, :])
                        last.then_inc(nat_made, 1)

                for half in range(2):
                    natural(0, half)
                with pe.Fori(1, 3) as kind:
                    for half in range(2):
                        natural(kind, half)

            @block.scalar
            def _(act):
                act.wait_ge(given, 80)
                act.activation(a_neg[:, :], small_rows[:, 1, :], ACT.Exp).then_inc(act_step, 1)
                act.wait_ge(dt_made, 1)
                act.wait_ge(x_split, 2 * KC)
                act.activation(low[:, :], low_ps[0:RANK, :], ACT.Copy).then_inc(low_ready, 1)
                act.wait_ge(dt_biased, 1)
                act.activation(dt_tmp[:, 1, :], dt_tmp[:, 0, :], ACT.Abs).then_inc(act_step, 1)
                act.wait_ge(act_step, 2)
                act.activation(dt_tmp[:, 1, :], dt_tmp[:, 1, :], ACT.Exp, scale=-1.0).then_inc(act_step, 1)
                act.wait_ge(act_step, 3)
                act.activation(dt_tmp[:, 1, :], dt_tmp[:, 1, :], ACT.Ln, bias=1.0).then_inc(dt_logged, 1)

                def gate(g):
                    act.wait_ge(gate_min, g + 1)
                    if g >= 2:
                        act.wait_ge(gate_sum, g - 1)
                    act.activation(conv[g % 2][:, :], low_ps[:, :], ACT.Abs,
                                   bias=small_cols[:, g:g + 1]).then_inc(act_step, 1)
                    act.wait_ge(act_step, 4 + 3 * g)
                    act.activation(conv[g % 2][:, :], conv[g % 2][:, :], ACT.Exp, scale=-1.0).then_inc(act_step, 1)
                    act.wait_ge(act_step, 5 + 3 * g)
                    act.activation(conv[g % 2][:, :], conv[g % 2][:, :], ACT.Ln, bias=1.0).then_inc(gate_log, 1)
                    act.wait_ge(gate_sum, g + 1)
                    if g >= 1:
                        act.wait_ge(stored[1], 16 * g)
                    act.activation(stage[1][:, :], padded[g % 2][:, CONV - 1:], ACT.Copy,
                                   scale=1.0 / GATE_TAU).then_inc(staged, 1)
                    act.wait_ge(staged, 2 * g + 2)
                    act.sem_inc(act_step, 1)

                def copy_out(i, j, scale):
                    act.wait_ge(tr_made, 2 * i + j + 1)
                    act.wait_ge(stored[j], 16 * (NG // 2 + i))
                    act.activation(stage[j][:, :], group[j][:, :], ACT.Copy, scale=scale).then_inc(staged, 1)
                    act.wait_ge(staged, NG + 2 * i + j + 1)
                    act.sem_inc(tr_read, 1)

                for g in range(NG):
                    act.wait_ge(tr_made, g + 1)
                    if g >= 1:
                        act.wait_ge(stored[0], 16 * g)
                    act.activation(stage[0][:, :], group[g % 2][:, :], ACT.Copy, scale=Q_SCALE).then_inc(staged, 1)
                    act.wait_ge(staged, 2 * g + 1)
                    act.sem_inc(tr_read, 1)
                    gate(g)
                act.wait_ge(cs_exp_in, 1)
                for what in (3, 4, 5):
                    last = act.activation(scalars[:, :, what, :], scalars[:, :, what, :], ACT.Exp)
                last.then_inc(cs_exp_out, 1)

                with act.Fori(GLA_BLOCKS // 2, GLA_BLOCKS) as i:
                    for j in range(2):
                        copy_out(i, j, 1.0)

                def convolved(i, j):
                    b = 2 * i + j
                    act.wait_ge(tr_made, NQK + b + 1)
                    act.activation(padded[j][:, CONV - 1:], group[j][:, :], ACT.Copy).then_inc(tr_read, 1)
                    act.wait_ge(conv_done, b + 1)
                    act.wait_ge(stored[j], 16 * ((NG + NQK) // 2 + i))
                    act.activation(stage[j][:, :], conv[j][:, :], ACT.Silu).then_inc(staged, 1)

                with act.Fori(0, XBC_BLOCKS // 2) as i:
                    for j in range(2):
                        convolved(i, j)

                def natural(kind, half, func):
                    for q in range(PAIRS):
                        count = (2 * kind + half) * PAIRS + q
                        act.wait_ge(nat_made, count + 1)
                        act.wait_ge(stored[q % 2], 16 * ((NG + NTR) // 2) + 32 * ((2 * kind + half) * (PAIRS // 2) + q // 2))
                        act.activation(stage[q % 2][:, :], group[q % 2][:, :], func).then_inc(staged, 1)
                        act.wait_ge(staged, NG + NTR + count + 1)
                        act.sem_inc(nat_read, 1)

                for half in range(2):
                    natural(0, half, ACT.Copy)
                with act.Fori(1, 3) as kind:
                    for half in range(2):
                        natural(kind, half, ACT.Silu)

            @block.vector
            def _(dve):
                dve.memset(ones[:, :], 1.0).then_inc(consts_made, 1)
                for j in range(2):
                    dve.memset(padded[j][:, 0:CONV - 1], 0.0).then_inc(consts_made, 1)
                for half in range(2):
                    dve.wait_ge(x_loaded[half], 64)
                    for k in range(4 * half, 4 * half + 4):
                        dve.tensor_copy(x_h[:, k, :], x_raw[k]).then_inc(x_split, 1)
                    dve.wait_ge(x_split, KC * half + 4)
                    for k in range(4 * half, 4 * half + 4):
                        dve.tensor_tensor(x_l[:, k, :], x_raw[k], x_h[:, k, :].bitcast(F32),
                                          ALU.subtract).then_inc(x_split, 1)
                dve.wait_ge(x_split, 2 * KC)
                dve.wait_ge(given, 80)
                dve.wait_ge(dt_made, 1)
                z3 = "p (t h) -> p t h"

                def per_head(row):
                    return row.unsqueeze(1).to_broadcast([P, TILES, HEADS_SSD])

                dve.tensor_tensor(dt_tmp[:, 0, :].rearrange(z3, h=HEADS_SSD),
                                  dt_ps[:, 0:TILES * HEADS_SSD].rearrange(z3, h=HEADS_SSD),
                                  per_head(small_rows[:, 0, :]), ALU.add).then_inc(dt_biased, 1)
                dve.memset(carry, 1.0).then_inc(dve_step, 1)
                dve.wait_ge(dve_step, 1)
                dve.memset(carry.rearrange("p (t u) -> p t u", u=P)[:, :, 0:1], 0.0).then_inc(consts_made, 1)
                dve.wait_ge(consts_made, 4)
                dve.wait_ge(dt_logged, 1)
                dve.wait_ge(dt_biased, 1)
                dve.scalar_tensor_tensor(dt_tmp[:, 2, :], dt_tmp[:, 0, :], 0.0, dt_tmp[:, 1, :], ALU.max,
                                         ALU.add).then_inc(dve_step, 1)
                dve.wait_ge(dve_step, 2)
                dt3 = dt_tmp[:, 2, :].rearrange(z3, h=HEADS_SSD)
                dve.tensor_copy(scalars[:, :, 1, :], dt3)
                dve.wait_ge(act_step, 1)
                dve.scalar_tensor_tensor(a_all[:, :].rearrange(z3, h=HEADS_SSD), dt3, -1.0,
                                         per_head(a_neg[:, :]), ALU.mult, ALU.mult).then_inc(a_ready, 1)
                dve.wait_ge(a_ready, 1)
                dve.tensor_copy(scalars[:, :, 0, :], a_all[:, :].rearrange(z3, h=HEADS_SSD))
                dve.wait_ge(cs_made, 1)
                cs = dt_ps[:, 512:512 + P].rearrange(z3, h=HEADS_SSD)
                total = dt_ps[:, 512 + P:512 + 2 * P].rearrange(z3, h=HEADS_SSD)
                dve.tensor_scalar(scalars[:, :, 2, :], cs, -1.0, None, ALU.mult)
                dve.tensor_copy(scalars[:, :, 3, :], cs)
                dve.tensor_copy(scalars[:, :, 5, :], total).then_inc(dve_step, 1)
                dve.wait_ge(dve_step, 3)
                dve.tensor_tensor(scalars[:, :, 4, :], scalars[:, :, 5, :], cs, ALU.subtract).then_inc(cs_exp_in, 1)
                for g in range(NG):
                    dve.wait_ge(gate_made, g + 1)
                    if g >= 2:
                        dve.wait_ge(staged, 2 * g - 2)
                    t = padded[g % 2][:, CONV - 1:]
                    dve.tensor_scalar(t, low_ps[:, :], small_cols[:, g:g + 1], 0.0, ALU.add, ALU.min).then_inc(gate_min, 1)
                    dve.wait_ge(gate_min, g + 1)
                    dve.wait_ge(gate_log, g + 1)
                    dve.tensor_tensor(t, t, conv[g % 2][:, :], ALU.subtract).then_inc(gate_read, 1)
                    dve.wait_ge(gate_read, g + 1)
                    dve.tensor_tensor_scan(t, carry, t, 0.0, ALU.mult, ALU.add).then_inc(gate_sum, 1)
                dve.wait_ge(cs_exp_out, 1)
                dve.tensor_tensor(scalars[:, :, 4, :], scalars[:, :, 4, :], scalars[:, :, 1, :],
                                  ALU.mult)
                dve.wait_ge(staged, 2 * NG)

                for b in range(XBC_BLOCKS):
                    j = b % 2
                    dve.wait_ge(tr_read, NQK + b + 1)
                    if b >= 2:
                        dve.wait_ge(staged, NG + NQK + b - 1)
                    dve.tensor_scalar(conv[j][:, :], padded[j][:, 0:SEQ], taps[:, CONV * b:CONV * b + 1],
                                      small_cols[:, GLA_BLOCKS + CONV * XBC_BLOCKS + b:GLA_BLOCKS + CONV * XBC_BLOCKS + b + 1],
                                      ALU.mult, ALU.add).then_inc(dve_step, 1)
                    for tap in range(1, CONV):
                        dve.wait_ge(dve_step, 3 + 3 * b + tap)
                        last = dve.scalar_tensor_tensor(conv[j][:, :], padded[j][:, tap:tap + SEQ],
                                                        taps[:, CONV * b + tap:CONV * b + tap + 1],
                                                        conv[j][:, :], ALU.mult, ALU.add)
                        last.then_inc(dve_step if tap < CONV - 1 else conv_done, 1)


def mix_tokens(nc, a, scanT_dram, nat_dram, scalars, h1_dram):
    with ExitStack() as ctx:
        sb, psum, sem = allocators(nc, ctx)
        w_out = sb("w_out", [P, 2 * KC, D], F32)
        ident = sb("ident2", [P, P], F32)
        tri = sb("tri2", [P, P], F32)
        ident16 = sb("ident16", [P, P], BF16)
        future16 = sb("future16", [P, P], BF16)
        level_mask = sb("level_mask", [P, LEVELS + 1, P], BF16)
        gainT = sb("gainT", [P, 2 * KC], F32)
        d_row = sb("d_row", [P, HEADS_SSD], F32)
        ln = sb("ln_rows1", [P, 2, D], F32)
        eps = sb("eps2", [P, 2], F32)
        qkb = sb("qkb", [P, 3, GLA_BLOCKS * P], F32)
        xsb = sb("xsb", [P, KC + 1, P], F32)
        cT = sb("cT", [P, 2, P], F32)
        v_in = sb("v_in", [P, D], F32)
        gate_in = sb("gate_in", [P, 2, D], F32)
        x_in = sb("x_in", [P, D], F32)
        expo = sb("expo", [P, LEVELS, GLA_BLOCKS * P], F32)
        q_lv = sb("q_lv", [P, LEVELS, GLA_BLOCKS * P], F32)
        k_lv = sb("k_lv", [P, LEVELS, GLA_BLOCKS * P], F32)
        q_in = sb("q_in", [P, GLA_BLOCKS * P], F32)
        k_end = sb("k_end", [P, GLA_BLOCKS * P], F32)
        exp_b = sb("exp_b", [P, GLA_BLOCKS * P], F32)
        exp_end = sb("exp_end", [P, GLA_BLOCKS * P], F32)
        b_last = sb("b_last", [P, 2, GLA_BLOCKS], F32)
        kb_nat = sb("kb_nat", [P, (GLA_BLOCKS + 1) * P], F32)
        masked = sb("masked", [P, (LEVELS + 1) * P], F32)
        att = sb("att", [P, GLA_BLOCKS, P], F32)
        state = sb("gla_state", [P, D], F32)
        hstate = sb("ssd_state", [P, 512], F32)
        scal = sb("scal", [P, 2, KINDS, HEADS_SSD], F32)
        xs = sb("xs", [P, D], F32)
        xdt = sb("xdt", [P, D], F32)
        xend = sb("xend", [P, D], F32)
        decay = sb("decay", [P, HEADS_SSD, P], F32)
        o_sb = sb("o_sb", [P, D], F32)
        y_sb = sb("y_sb", [P, D], F32)
        mixT = sb("mixT", [P, 2 * KC, P], F32)
        stats = sb("stats1", [P, 2, 6], F32)
        moments = sb("moments1", [P, 2], F32)
        lstd = sb("lstd", [P, 2], F32)
        ms = sb("ms", [P, 3, 8], F32)
        bank = [psum(f"mix_bank{i}", [P, D], F32) for i in range(4)]
        A, B, C, Dk = bank
        place = dict(X=A, L0=B, L1=C, KB=Dk, L2=A, L3=B, CB=C, CS0=Dk, CS1=A, OTa=B, OTb=Dk, OUT=B,
                     O=A, SN=Dk, YO=A, YD=C, HN=Dk)
        made = {k: sem(f"made_{k}") for k in place}
        read = {k: sem(f"read_{k}") for k in place}
        consts = sem("consts2")
        wout_loaded = sem("wout_loaded")
        zeros_made, eps_made = sem("zeros_made"), sem("eps2_made")
        qkb_loaded, xsb_loaded, v_loaded, gate_loaded, x_loaded = (
            sem("qkb_loaded"), sem("xsb_loaded"), sem("v_loaded"), sem("gate_loaded"), sem("x2_loaded"))
        cT_loaded = [sem(f"cT_loaded{i}") for i in range(2)]
        scal_ready = sem("scal_ready")
        expo_in, expo_out, levels_ready = sem("expo_in"), sem("expo_out"), sem("levels_ready")
        prep_step, dve_step, act_step = sem("prep_step"), sem("dve2_step"), sem("act2_step")
        xdt_ready, decay_ready, skip_ready = sem("xdt_ready"), sem("decay_ready"), sem("skip_ready")
        o_root, y_root, y_gated, og_ready, yg_ready = (
            sem("o_root"), sem("y_root"), sem("y_gated"), sem("og_ready"), sem("yg_ready"))
        state_ready, hstate_ready = sem("state_ready"), sem("hstate_ready")
        var_ready, root_ready, h1_ready, h1_stored = sem("var1"), sem("root1"), sem("h1_ready2"), sem("h1_stored")
        passed, sp_passed = sem("dve2_waits_passed"), sem("sp2_waits_passed")
        att_ready = sem("att_ready")
        norm_step = sem("norm1_step")
        CONSTS = 8 * 16
        skip = masked

        def tiles(engine, body):
            body(0, 0)
            with engine.Fori(0, (TILES - 2) // 2) as i:
                body(2 * i + 1, 1)
                body(2 * i + 2, 0)
            body(TILES - 1, 1)

        def first(t):
            return isinstance(t, int) and t == 0

        def final(t):
            return isinstance(t, int) and t == TILES - 1

        with nc.Block() as block:
            @block.sync
            def _(sp):
                def load_qkb(t):
                    for w, b0 in enumerate((0, GLA_BLOCKS, 2 * GLA_BLOCKS + XBC_BLOCKS)):
                        sp.dma_start(qkb[:, w, :].rearrange("p (b u) -> p b u", u=P),
                                     scanT_dram[b0:b0 + GLA_BLOCKS, :, bass.ts(t, P)].rearrange("b p u -> p b u")
                                     ).then_inc(qkb_loaded, 16)

                def load_xsb(t):
                    b0 = 2 * GLA_BLOCKS
                    sp.dma_start(xsb[:, :, :], scanT_dram[b0:b0 + KC + 1, :, bass.ts(t, P)].rearrange("b p u -> p b u")
                                 ).then_inc(xsb_loaded, 16)

                def load_cT(t, s):
                    sp.dma_start(cT[:, s, :], scanT_dram[2 * GLA_BLOCKS + KC + 1, :, bass.ts(t, P)]
                                 ).then_inc(cT_loaded[s], 16)

                def load_v(t):
                    sp.dma_start(v_in[:, :], nat_dram[0, t]).then_inc(v_loaded, 16)

                def load_gates(t):
                    for g in range(2):
                        sp.dma_start(gate_in[:, g, :], nat_dram[1 + g, t]).then_inc(gate_loaded, 16)

                def load_x(t):
                    sp.dma_start(x_in[:, :], a["x"][t]).then_inc(x_loaded, 16)

                load_qkb(0)
                load_xsb(0)
                load_cT(0, 0)
                load_v(0)
                for dst, name in ((ident[:, :], "ident"), (tri[:, :], "tri"), (ident16[:, :], "ident16"), (future16[:, :], "future16"),
                                  (level_mask[:, :, :], "level_mask"), (gainT[:, :], "gainT"),
                                  (d_row[:, :], "d_row"), (ln[:, :, :], "ln1")):
                    sp.dma_start(dst, a[name]).then_inc(consts, 16)
                load_gates(0)
                load_x(0)

                def body(t, s):
                    if not final(t):
                        sp.wait_ge(made["CB"], t + 1)
                        load_xsb(t + 1)
                        sp.wait_ge(made["L3"], t + 1)
                        sp.sem_inc(sp_passed, 1)
                        load_qkb(t + 1)
                        load_cT(t + 1, 1 - s)
                    if first(t):
                        sp.dma_start(w_out[:, :, :], a["w_out"]).then_inc(wout_loaded, 16)
                    if not final(t):
                        sp.wait_ge(made["SN"], t + 1)
                        load_v(t + 1)
                        sp.wait_ge(yg_ready, t + 1)
                        load_gates(t + 1)
                    if not first(t):
                        sp.wait_ge(h1_ready, t)
                        sp.dma_start(h1_dram[t - 1], x_in[:, :]).then_inc(h1_stored, 16)
                        sp.wait_ge(h1_stored, 16 * t)
                        load_x(t)

                tiles(sp, body)
                sp.wait_ge(h1_ready, TILES)
                sp.dma_start(h1_dram[TILES - 1], x_in[:, :]).then_inc(h1_stored, 16)
                sp.wait_ge(h1_stored, 16 * TILES)

            @block.gpsimd
            def _(pool):
                pool.memset(q_lv[:, :, :], 0.0).then_inc(zeros_made, 1)
                pool.memset(k_lv[:, :, :], 0.0).then_inc(zeros_made, 1)

            @block.tensor
            def _(pe):
                pe.wait_ge(consts, CONSTS)
                pe.wait_ge(zeros_made, 4)

                def turned(t, part):
                    src, ready = (o_sb, og_ready) if part == "OTa" else (y_sb, yg_ready)
                    pe.wait_ge(ready, t + 1)
                    for k in range(KC):
                        last = pe.transpose(place[part][:, k * P:(k + 1) * P], src[:, k * P:(k + 1) * P],
                                            ident[:, :])
                    last.then_inc(made[part], 1)

                def project(t, quarter):
                    if quarter == 0:
                        pe.wait_ge(wout_loaded, 16)
                        pe.wait_ge(read["OTa"], t + 1)
                        pe.wait_ge(read["OTb"], t + 1)
                    c, k0 = quarter // 2, quarter % 2 * KC
                    for k in range(k0, k0 + KC):
                        last = pe.matmul(place["OUT"][:, c * 512:(c + 1) * 512], mixT[:, k, :],
                                         w_out[:, k, c * 512:(c + 1) * 512], start=(k == 0), stop=(k == 2 * KC - 1))
                    if quarter == 3:
                        last.then_inc(made["OUT"], 1)

                def decays(t, s, g):
                    part = f"CS{g}"
                    for c in range(2):
                        pe.matmul(place[part][:, c * 512:(c + 1) * 512], ident16[:, :],
                                  future16[:, :].unsqueeze(1).to_broadcast([P, 4, P]),
                                  start=True, stop=False, skip_group_check=True)
                        for q in range(4):
                            h = 8 * g + 4 * c + q
                            last = pe.matmul(place[part][:, c * 512 + q * P:c * 512 + (q + 1) * P],
                                             scal[:, s, 0, h:h + 1].to_broadcast([P, P]), tri[:, :],
                                             start=False, stop=(q == 3), skip_group_check=True)
                    last.then_inc(made[part], 1)

                def levels(t, h):
                    part = f"L{h}"
                    cols = slice(h * P, (h + 1) * P)
                    for lv in range(LEVELS + 1):
                        kk = k_lv[:, lv, cols] if lv < LEVELS else qkb[:, 1, cols]
                        qq = q_lv[:, lv, cols] if lv < LEVELS else qkb[:, 0, cols]
                        last = pe.matmul(place[part][:, lv * P:(lv + 1) * P], kk, qq, start=True, stop=True)
                    last.then_inc(made[part], 1)

                def body(t, s):
                    pe.wait_ge(xsb_loaded, 16 * (t + 1))
                    if not first(t):
                        pe.wait_ge(read["YO"], t)
                    for k in range(KC):
                        last = pe.transpose(place["X"][:, k * P:(k + 1) * P], xsb[:, k, :], ident[:, :])
                    last.then_inc(made["X"], 1)
                    pe.wait_ge(levels_ready, t + 1)
                    if not first(t):
                        pe.wait_ge(read["OUT"], t)
                        pe.wait_ge(read["YD"], t)
                        pe.wait_ge(read["HN"], t)
                    levels(t, 0)
                    levels(t, 1)
                    for h in range(GLA_BLOCKS):
                        pe.transpose(place["KB"][:, h * P:(h + 1) * P], k_end[:, h * P:(h + 1) * P], ident[:, :])
                    pe.transpose(place["KB"][:, 512:512 + P], xsb[:, KC, :], ident[:, :]).then_inc(made["KB"], 1)
                    pe.wait_ge(read["X"], t + 1)
                    levels(t, 2)
                    pe.wait_ge(read["L0"], t + 1)
                    levels(t, 3)
                    pe.wait_ge(read["L1"], t + 1)
                    pe.wait_ge(cT_loaded[s], 8 * (t - s) + 16)
                    for g in range(2):
                        rows = slice(64 * g, 64 * g + 64)
                        last = pe.matmul(place["CB"][:, g * 512:g * 512 + P], xsb[rows, KC, :], cT[rows, s, :],
                                         start=True, stop=True)
                    last.then_inc(made["CB"], 1)
                    if not first(t):
                        pe.wait_ge(read["KB"], t + 1)
                        turned(t - 1, "OTb")
                    pe.wait_ge(scal_ready, t + 1)
                    pe.wait_ge(read["L2"], t + 1)
                    decays(t, s, 1)
                    if not first(t):
                        pe.wait_ge(read["L3"], t + 1)
                        turned(t - 1, "OTa")
                        pe.wait_ge(read["OTb"], t)
                    else:
                        pe.wait_ge(read["KB"], 1)
                    decays(t, s, 0)
                    pe.wait_ge(read["CS1"], t + 1)
                    pe.wait_ge(att_ready, GLA_BLOCKS * (t + 1))
                    pe.wait_ge(v_loaded, 16 * (t + 1))
                    if not first(t):
                        pe.wait_ge(state_ready, t)
                    for h in range(GLA_BLOCKS):
                        e = slice(h * 256, (h + 1) * 256)
                        pe.matmul(place["O"][:, e], q_in[:, h * P:(h + 1) * P], state[:, e], start=True, stop=False)
                        last = pe.matmul(place["O"][:, e], att[:, h, :], v_in[:, e], start=False, stop=True)
                    last.then_inc(made["O"], 1)
                    if not first(t):
                        project(t - 1, 0)
                    pe.wait_ge(read["CS0"], t + 1)
                    for h in range(GLA_BLOCKS):
                        e = slice(h * 256, (h + 1) * 256)
                        last = pe.matmul(place["SN"][:, e], kb_nat[:, h * P:(h + 1) * P], v_in[:, e],
                                         start=True, stop=True)
                    last.then_inc(made["SN"], 1)
                    pe.wait_ge(decay_ready, t + 1)
                    pe.wait_ge(skip_ready, t + 1)
                    for c in range(2):
                        pe.matmul(place["YD"][:, c * 512:(c + 1) * 512], ident[:, :], skip[:, c * 512:(c + 1) * 512],
                                  start=True, stop=False, skip_group_check=True)
                        for q in range(8):
                            h = 8 * c + q
                            last = pe.matmul(place["YD"][:, h * 64:(h + 1) * 64], decay[:, h, :],
                                             xdt[:, h * 64:(h + 1) * 64], start=False, stop=(q == 7),
                                             skip_group_check=True)
                    last.then_inc(made["YD"], 1)
                    if not first(t):
                        project(t - 1, 1)
                    pe.wait_ge(read["O"], t + 1)
                    if not first(t):
                        pe.wait_ge(hstate_ready, t)
                    for g in range(2):
                        rows = slice(64 * g, 64 * g + 64)
                        last = pe.matmul(place["YO"][:, g * 512:(g + 1) * 512], cT[rows, s, :], hstate[rows, :],
                                         start=True, stop=True)
                    last.then_inc(made["YO"], 1)
                    if not first(t):
                        project(t - 1, 2)
                        project(t - 1, 3)
                    pe.wait_ge(read["SN"], t + 1)
                    for g in range(2):
                        last = pe.matmul(place["HN"][:, g * 512:(g + 1) * 512], kb_nat[:, 512:512 + P],
                                         xend[:, g * 512:(g + 1) * 512], start=True, stop=True)
                    last.then_inc(made["HN"], 1)

                tiles(pe, body)
                pe.wait_ge(read["OUT"], TILES)
                turned(TILES - 1, "OTa")
                pe.wait_ge(read["HN"], TILES)
                turned(TILES - 1, "OTb")
                for quarter in range(4):
                    project(TILES - 1, quarter)

            @block.scalar
            def _(act):

                def exponentials(t, s):
                    act.wait_ge(expo_in, t + 1)
                    act.activation(expo[:, :, :].rearrange("p l u -> p (l u)"),
                                   expo[:, :, :].rearrange("p l u -> p (l u)"), ACT.Exp)
                    act.activation(exp_end[:, :], exp_end[:, :], ACT.Exp)
                    act.activation(exp_b[:, :], qkb[:, 2, :], ACT.Exp)
                    act.activation(b_last[:, s, :], qkb[:, 2, :].rearrange("p (h u) -> p h u", u=P)[:, :, P - 1],
                                   ACT.Exp).then_inc(expo_out, 1)

                def body(t, s):
                    act.wait_ge(made["X"], t + 1)
                    if not first(t):
                        act.wait_ge(skip_ready, t)
                    act.activation(xs[:, :], place["X"][:, :], ACT.Copy).then_inc(read["X"], 1)
                    act.wait_ge(made["KB"], t + 1)
                    if not first(t):
                        act.wait_ge(made["HN"], t)
                    act.activation(kb_nat[:, :], place["KB"][:, 0:5 * P], ACT.Copy).then_inc(read["KB"], 1)
                    act.wait_ge(scal_ready, t + 1)
                    if not first(t):
                        turned_scaled(t, "OTb")
                    decay_of(t, s, 1)
                    if not first(t):
                        turned_scaled(t, "OTa")
                    decay_of(t, s, 0)
                    if not final(t):
                        exponentials(t + 1, 1 - s)
                    act.wait_ge(made["O"], t + 1)
                    for h in range(GLA_BLOCKS):
                        e = slice(h * 256, (h + 1) * 256)
                        last = act.activation(o_sb[:, e], place["O"][:, e], ACT.Square, accum_out=ms[:, 0, h:h + 1])
                    last.then_inc(act_step, 1)
                    act.wait_ge(act_step, 2 * t + 1)
                    act.activation(ms[:, 1, 0:4], ms[:, 0, 0:4], ACT.Sqrt, scale=1.0 / 256,
                                   bias=eps[:, 1:2]).then_inc(o_root, 1)
                    act.wait_ge(y_gated, t + 1)
                    for g in range(2):
                        e = slice(g * 512, (g + 1) * 512)
                        last = act.activation(xs[:, e], y_sb[:, e], ACT.Square, accum_out=ms[:, 0, 4 + g:5 + g])
                    last.then_inc(act_step, 1)
                    act.wait_ge(act_step, 2 * t + 2)
                    act.activation(ms[:, 1, 4:6], ms[:, 0, 4:6], ACT.Sqrt, scale=1.0 / 512,
                                   bias=eps[:, 1:2]).then_inc(y_root, 1)
                    if not first(t):
                        root_of_norm(t)

                def decay_of(t, s, g):
                    part = f"CS{g}"
                    act.wait_ge(made[part], t + 1)
                    for q in range(8):
                        h = 8 * g + q
                        last = act.activation(decay[:, h, :], place[part][:, q * P:(q + 1) * P], ACT.Exp,
                                              bias=scal[:, s, 2, h:h + 1])
                    last.then_inc(read[part], 1)

                def turned_scaled(t, part):
                    j = KC if part == "OTb" else 0
                    act.wait_ge(made[part], t)
                    for k in range(KC):
                        last = act.activation(mixT[:, j + k, :], place[part][:, k * P:(k + 1) * P],
                                              ACT.Copy, scale=gainT[:, j + k:j + k + 1])
                    last.then_inc(read[part], 1)

                def root_of_norm(t):
                    act.wait_ge(var_ready, t)
                    act.activation(lstd[:, 0:1], moments[:, 1:2], ACT.Sqrt, bias=eps[:, 0:1]).then_inc(root_ready, 1)

                exponentials(0, 0)
                act.wait_ge(consts, CONSTS)
                act.wait_ge(eps_made, 2)
                tiles(act, body)
                turned_scaled(TILES, "OTa")
                turned_scaled(TILES, "OTb")
                root_of_norm(TILES)

            @block.vector
            def _(dve):
                dve.memset(state[:, :], 0.0).then_inc(zeros_made, 1)
                dve.memset(hstate[:, :], 0.0).then_inc(zeros_made, 1)
                dve.memset(eps[:, 0:1], LN_EPS).then_inc(eps_made, 1)
                dve.memset(eps[:, 1:2], RMS_EPS).then_inc(eps_made, 1)
                dve.sem_inc(read["OUT"], 1)
                def pairs(x, lv):
                    return x.rearrange("p (n two m) -> p n two m", two=2, m=1 << lv)

                def exponents(t):
                    dve.wait_ge(qkb_loaded, 48 * (t + 1))
                    for lv in range(LEVELS):
                        b, e = pairs(qkb[:, 2, :], lv), pairs(expo[:, lv, :], lv)
                        m = 1 << lv
                        ref = b[:, :, 0, m - 1:m].to_broadcast([P, GLA_BLOCKS * P // (2 * m), m])
                        dve.tensor_tensor(e[:, :, 0, :], ref, b[:, :, 0, :], ALU.subtract)
                        dve.tensor_tensor(e[:, :, 1, :], b[:, :, 1, :], ref, ALU.subtract)
                    b = qkb[:, 2, :].rearrange("p (h u) -> p h u", u=P)
                    dve.tensor_tensor(exp_end[:, :].rearrange("p (h u) -> p h u", u=P),
                                      b[:, :, P - 1:P].to_broadcast([P, GLA_BLOCKS, P]), b,
                                      ALU.subtract).then_inc(expo_in, 1)

                def level_operands(t):
                    dve.wait_ge(expo_out, t + 1)
                    if not first(t):
                        dve.wait_ge(made["O"], t)
                    for lv in range(LEVELS):
                        e = pairs(expo[:, lv, :], lv)
                        dve.tensor_tensor(pairs(q_lv[:, lv, :], lv)[:, :, 1, :], pairs(qkb[:, 0, :], lv)[:, :, 1, :],
                                          e[:, :, 1, :], ALU.mult)
                        dve.tensor_tensor(pairs(k_lv[:, lv, :], lv)[:, :, 0, :], pairs(qkb[:, 1, :], lv)[:, :, 0, :],
                                          e[:, :, 0, :], ALU.mult)
                    dve.tensor_tensor(q_in[:, :], qkb[:, 0, :], exp_b[:, :], ALU.mult)
                    dve.tensor_tensor(k_end[:, :], qkb[:, 1, :], exp_end[:, :], ALU.mult).then_inc(levels_ready, 1)

                def norm_first(t):
                    dve.wait_ge(made["OUT"], t)
                    dve.wait_ge(x_loaded, 16 * t)
                    dve.scalar_tensor_tensor(x_in[:, :], x_in[:, :], ALPHA, place["OUT"][:, :], ALU.mult,
                                             ALU.add).then_inc(read["OUT"], 1)
                    dve.wait_ge(read["OUT"], t + 1)
                    for c in range(2):
                        last = dve.bn_stats(stats[:, c, :], x_in[:, c * 512:(c + 1) * 512])
                    last.then_inc(norm_step, 1)
                    dve.wait_ge(norm_step, 4 * (t - 1) + 1)
                    dve.sem_inc(passed, 1)
                    dve.bn_aggr(moments[:, :], stats[:, :, :].rearrange("p c s -> p (c s)")).then_inc(var_ready, 1)

                def norm_second(t):
                    at = 4 * (t - 1) + 1
                    dve.wait_ge(root_ready, t)
                    dve.reciprocal(lstd[:, 1:2], lstd[:, 0:1]).then_inc(norm_step, 1)
                    dve.wait_ge(norm_step, at + 1)
                    dve.tensor_scalar(x_in[:, :], x_in[:, :], moments[:, 0:1], lstd[:, 1:2], ALU.subtract,
                                      ALU.mult).then_inc(norm_step, 1)
                    dve.wait_ge(norm_step, at + 2)
                    dve.tensor_tensor(x_in[:, :], x_in[:, :], ln[:, 0, :], ALU.mult).then_inc(norm_step, 1)
                    dve.wait_ge(norm_step, at + 3)
                    dve.tensor_tensor(x_in[:, :], x_in[:, :], ln[:, 1, :], ALU.add).then_inc(h1_ready, 1)

                def body(t, s):
                    done = [0]

                    def link(ins):
                        done[0] += 1
                        ins.then_inc(dve_step, 1)
                        dve.wait_ge(dve_step, MIX_STEPS * t + done[0])

                    def heads(x, w):
                        return x.rearrange("p (h w) -> p h w", w=w)

                    def each(kind, width, rows=slice(0, P), hs=slice(0, HEADS_SSD)):
                        n = rows.stop - rows.start
                        return scal[rows, s, kind, hs].unsqueeze(2).to_broadcast([n, hs.stop - hs.start, width])

                    dve.tensor_copy(scal[:, s, :, :], scalars[:, bass.ds(t, 1), :, :].rearrange("p t k h -> p (t k) h")
                                    ).then_inc(scal_ready, 1)
                    dve.wait_ge(scal_ready, t + 1)
                    dve.wait_ge(read["X"], t + 1)
                    if not first(t):
                        dve.wait_ge(made["HN"], t)
                    dve.tensor_tensor(heads(xdt[:, :], 64), heads(xs[:, :], 64), each(1, 64), ALU.mult)
                    dve.tensor_tensor(heads(xend[:, :], 64), heads(xs[:, :], 64), each(4, 64), ALU.mult)
                    for h in range(GLA_BLOCKS):
                        dve.wait_ge(made[f"L{h}"], t + 1)
                        dve.tensor_tensor(masked[:, :], place[f"L{h}"][:, :],
                                          level_mask[:, :, :].rearrange("p l u -> p (l u)"),
                                          ALU.mult).then_inc(read[f"L{h}"], 1)
                        dve.wait_ge(read[f"L{h}"], t + 1)
                        dve.tensor_reduce(att[:, h, :], masked[:, :].rearrange("p (l u) -> p u l", u=P),
                                          AX, ALU.add).then_inc(att_ready, 1)
                        dve.wait_ge(att_ready, GLA_BLOCKS * t + h + 1)
                    dve.tensor_tensor(heads(skip[:, :], 64), heads(xs[:, :], 64),
                                      d_row[:, :].unsqueeze(2).to_broadcast([P, HEADS_SSD, 64]),
                                      ALU.mult).then_inc(skip_ready, 1)
                    if not final(t):
                        exponents(t + 1)
                    for g in (1, 0):
                        dve.wait_ge(read[f"CS{g}"], t + 1)
                        part = decay[:, 8 * g:8 * g + 8, :]
                        last = dve.tensor_tensor(part, part, place["CB"][:, g * 512:g * 512 + P].unsqueeze(1)
                                                 .to_broadcast([P, 8, P]), ALU.mult)
                    last.then_inc(decay_ready, 1)
                    dve.wait_ge(o_root, t + 1)
                    link(dve.reciprocal(ms[:, 2, 0:4], ms[:, 1, 0:4]))
                    dve.wait_ge(gate_loaded, 32 * (t + 1))
                    for h in range(GLA_BLOCKS):
                        e = slice(h * 256, (h + 1) * 256)
                        last = dve.scalar_tensor_tensor(o_sb[:, e], place["O"][:, e], ms[:, 2, h:h + 1],
                                                        gate_in[:, 0, e], ALU.mult, ALU.mult)
                    last.then_inc(og_ready, 1)
                    dve.wait_ge(og_ready, t + 1)
                    dve.sem_inc(read["O"], 1)
                    dve.wait_ge(made["SN"], t + 1)
                    for h in range(GLA_BLOCKS):
                        e = slice(h * 256, (h + 1) * 256)
                        last = dve.scalar_tensor_tensor(state[:, e], state[:, e], b_last[:, s, h:h + 1],
                                                        place["SN"][:, e], ALU.mult, ALU.add)
                    last.then_inc(state_ready, 1)
                    dve.wait_ge(state_ready, t + 1)
                    dve.sem_inc(read["SN"], 1)
                    if not final(t):
                        level_operands(t + 1)
                    dve.wait_ge(made["YO"], t + 1)
                    dve.tensor_tensor(heads(y_sb[:, :], 64), heads(place["YO"][:, :], 64), each(3, 64),
                                      ALU.mult).then_inc(read["YO"], 1)
                    dve.wait_ge(read["YO"], t + 1)
                    dve.tensor_tensor(y_sb[:, :], y_sb[:, :], place["YD"][:, :], ALU.add).then_inc(read["YD"], 1)
                    dve.wait_ge(read["YD"], t + 1)
                    dve.tensor_tensor(y_sb[:, :], y_sb[:, :], gate_in[:, 1, :], ALU.mult).then_inc(y_gated, 1)
                    if not first(t):
                        norm_first(t)
                    dve.wait_ge(made["HN"], t + 1)
                    sides = [slice(64 * g, 64 * g + 64) for g in range(2)]
                    for g, rows in enumerate(sides):
                        last = dve.tensor_tensor(heads(hstate[rows, :], 64), heads(hstate[rows, :], 64),
                                                 each(5, 64, rows, slice(8 * g, 8 * g + 8)), ALU.mult)
                    link(last)
                    for g, rows in enumerate(sides):
                        last = dve.tensor_tensor(hstate[rows, :], hstate[rows, :],
                                                 place["HN"][rows, g * 512:(g + 1) * 512], ALU.add)
                    last.then_inc(hstate_ready, 1)
                    dve.wait_ge(hstate_ready, t + 1)
                    dve.sem_inc(read["HN"], 1)
                    dve.wait_ge(y_root, t + 1)
                    link(dve.reciprocal(ms[:, 2, 4:6], ms[:, 1, 4:6]))
                    for g in range(2):
                        e = slice(g * 512, (g + 1) * 512)
                        last = dve.tensor_scalar(y_sb[:, e], y_sb[:, e], ms[:, 2, 4 + g:5 + g], None, ALU.mult)
                    last.then_inc(yg_ready, 1)
                    if not first(t):
                        norm_second(t)
                    assert done[0] == MIX_STEPS

                exponents(0)
                dve.wait_ge(zeros_made, 4)
                level_operands(0)
                dve.wait_ge(consts, CONSTS)
                tiles(dve, body)
                norm_first(TILES)
                norm_second(TILES)


def retrieval_constants(sb, sem):
    return dict(pwq=sb("pwq", [P, KC, D], F32), keys=sb("keys", [P, NKEYS], F32), ident=sb("ident3", [P, P], F32),
                iota16=sb("iota16", [P, TOPK], F32), ln=sb("ln_rows3", [P, 4, D], F32), h1=sb("h1_tile", [P, D], F32),
                consts_loaded=sem("consts3_loaded"), pwq_loaded=sem("pwq_loaded"), h1_loaded=sem("h1_loaded"))


def build_memory_tables(nc, a, h1_dram, mem_scores_w, mem_values_w, kept):
    with ExitStack() as ctx:
        sb, psum, sem = allocators(nc, ctx)
        mem_sb = sb("mem_sb", [P, KC, MEM], F32)
        weights = [sb(f"mem_weight{i}", [P, KC, D], F32) for i in range(2)]
        keysT = sb("keysT", [P, KC, MEM], F32)
        valuesT = sb("valuesT", [P, KC, MEM], F32)
        groups = [psum(f"mem_group{i}", [P, D], F32) for i in range(4)]
        N_PIECES = 2
        piece_loaded = [[sem(f"mem_piece_loaded{i}_{b}") for b in range(N_PIECES)] for i in range(2)]
        group_done = sem("mem_group_done")
        group_copied = sem("mem_group_copied")
        CB = KC // HEADS_CA
        GROUP_BLOCKS = D // MEM
        N_PROJ = KC // GROUP_BLOCKS

        def destination(g):
            if g < 2 * N_PROJ:
                t = keysT if g < N_PROJ else valuesT
                b = (g % N_PROJ) * GROUP_BLOCKS
                return t[:, b:b + GROUP_BLOCKS, :].rearrange("p b m -> p (b m)")
            t = mem_scores_w if g < 2 * N_PROJ + KC else mem_values_w
            return t[:, (g - 2 * N_PROJ) % KC, :]

        with nc.Block() as block:
            @block.sync
            def _(sp):
                sp.dma_start(mem_sb[:, :, :], a["memT"]).then_inc(piece_loaded[0][0], 16)
                for i, name in enumerate(("wk", "wv")):
                    for b in range(N_PIECES):
                        cols = slice(b * D // N_PIECES, (b + 1) * D // N_PIECES)
                        sp.dma_start(weights[i][:, :, cols], a[name][:, :, cols]).then_inc(piece_loaded[i][b], 16)
                sp.wait_ge(group_done, N_PROJ)
                sp.dma_start(weights[0][:, :, :], a["wqT"]).then_inc(piece_loaded[0][-1], 16)
                sp.wait_ge(group_done, 2 * N_PROJ)
                sp.dma_start(weights[1][:, :, :], a["wo"]).then_inc(piece_loaded[1][-1], 16)
                for dst, src in ((kept["ident"][:, :], a["ident"]), (kept["iota16"][:, :], a["iota"]),
                                 (kept["ln"][:, :, :], a["ln"]), (kept["keys"][:, :], a["keysT"])):
                    sp.dma_start(dst, src).then_inc(kept["consts_loaded"], 16)
                sp.dma_start(kept["h1"][:, :], h1_dram[0]).then_inc(kept["h1_loaded"], 16)
                sp.dma_start(kept["pwq"][:, :, :], a["peer_wq"]).then_inc(kept["pwq_loaded"], 16)

            @block.tensor
            def _(pe):
                for g in range(2 * N_PROJ):
                    for b in range(GROUP_BLOCKS):
                        c = (g % N_PROJ) * GROUP_BLOCKS + b
                        if c % (KC // N_PIECES) == 0:
                            pe.wait_ge(piece_loaded[g // N_PROJ][c * N_PIECES // KC], 32 if c + g == 0 else 16)
                        for k in range(KC):
                            last = pe.matmul(groups[g % 4][:, b * MEM:(b + 1) * MEM],
                                             weights[g // N_PROJ][:, k, c * P:(c + 1) * P], mem_sb[:, k, :],
                                             start=(k == 0), stop=(k == KC - 1))
                    last.then_inc(group_done, 1)
                for g in range(2 * N_PROJ, 2 * N_PROJ + 2 * KC):
                    pe.wait_ge(group_copied, g - 3)
                    r = (g - 2 * N_PROJ) % KC
                    if g < 2 * N_PROJ + KC:
                        if r == 0:
                            pe.wait_ge(group_copied, N_PROJ)
                            pe.wait_ge(piece_loaded[0][-1], 32)
                        for h in range(HEADS_CA):
                            for c in range(CB):
                                last = pe.matmul(groups[g % 4][:, h * MEM:(h + 1) * MEM],
                                                 weights[0][:, CB * h + c, r * P:(r + 1) * P],
                                                 keysT[:, CB * h + c, :], start=(c == 0), stop=(c == CB - 1))
                    else:
                        if r == 0:
                            pe.wait_ge(group_copied, 2 * N_PROJ)
                            pe.wait_ge(piece_loaded[1][-1], 32)
                        h, mb = r // 2, r % 2
                        for n in range(2):
                            for c in range(CB):
                                last = pe.matmul(groups[g % 4][:, n * 512:(n + 1) * 512],
                                                 valuesT[:, CB * h + c, mb * P:(mb + 1) * P],
                                                 weights[1][:, CB * h + c, n * 512:(n + 1) * 512],
                                                 start=(c == 0), stop=(c == CB - 1))
                    last.then_inc(group_done, 1)

            @block.scalar
            def _(act):
                for g in range(2 * N_PROJ + 2 * KC):
                    act.wait_ge(group_done, g + 1)
                    act.activation(destination(g), groups[g % 4][:, :], ACT.Copy).then_inc(group_copied, 1)


def attend_and_retrieve(nc, h1_dram, peer_u, peer_v, out, mem_scores_w, mem_values_w, kept):
    with ExitStack() as ctx:
        sb, psum, sem = allocators(nc, ctx)
        pwq, keys, ident, iota16, ln, h1, consts_loaded, pwq_loaded, h1_loaded = (
            kept[k] for k in ("pwq", "keys", "ident", "iota16", "ln", "h1", "consts_loaded", "pwq_loaded", "h1_loaded"))
        eps = sb("eps3", [P, 1], F32)
        h2 = sb("h2", [P, 2, D], F32)
        hT = sb("hT3", [P, KC, P], F32)
        pqT = sb("pqT", [P, PHEADS, P], F32)
        work = sb("work3", [P, 4 * D], F32)
        probs = work[:, 0:D]
        probsT = work[:, D:2 * D]
        pre2 = work[:, 2 * D:3 * D]
        scores = work[:, 0:2 * D]
        scores_cut = work[:, 2 * D:4 * D]
        y3 = sb("y3", [P, D], F32)
        u_ring = sb("u_ring", [P, RING, D], F32)
        v_ring = sb("v_ring", [P, RING, D], F32)
        diag = sb("diag", [P, RING, P], F32)
        idx = sb("idx", [P, 2, PICKS], mybir.dt.int32)
        gates = sb("gates", [P, 2, PICKS], F32)
        act_u = sb("act_u", [P, 2, TOPK], F32)
        gelu_u = sb("gelu_u", [P, 2, TOPK], F32)
        w_v = sb("w_v", [P, 2, TOPK], F32)
        vals = sb("vals", [P, 2 * PHEADS, TOPK], F32)
        vidx = sb("vidx", [P, 2 * PHEADS, TOPK], U32)
        vidx_f = sb("vidx_f", [P, 2 * PHEADS, TOPK], F32)
        best = sb("best", [P, PHEADS, TOPK], F32)
        bidx = sb("bidx", [P, PHEADS, TOPK], U32)
        bhalf = sb("bhalf", [P, 2, PICKS], U32)
        bhalf_f = sb("bhalf_f", [P, 2, PICKS], F32)
        ihalf = sb("ihalf", [P, 2, PICKS], F32)
        gexp = sb("gexp", [P, PHEADS, TOPK], F32)
        gsum = sb("gsum", [P, PHEADS], F32)
        ginv = sb("ginv", [P, PHEADS], F32)
        negmax = sb("negmax", [P, HEADS_CA], F32)
        rowmax = sb("rowmax", [P, HEADS_CA], F32)
        psums = sb("prob_sums", [P, HEADS_CA], F32)
        pinv = sb("prob_inv", [P, HEADS_CA], F32)
        stats = sb("stats3", [P, 2, 2, 6], F32)
        moments = sb("moments3", [P, 2, 2], F32)
        std = sb("std3", [P, 2], F32)
        rstd = sb("rstd3", [P, 2], F32)

        acc = psum("acc", [P, D], F32)
        small = psum("small3", [P, D], F32)
        wide = psum("wide3", [P, 2 * D], F32)

        u_landed = [sem(f"u_landed{i}") for i in range(RING)]
        v_landed = [sem(f"v_landed{i}") for i in range(RING)]
        dot_done = sem("dot_done")
        gelu_done = sem("gelu_done")
        w_ready = sem("w_ready")
        diag_ready = sem("diag_ready")
        v_used = sem("v_used")
        acc_copied = sem("acc_copied")
        y3_ready = sem("y3_ready")
        y3_stored, y3_free = sem("y3_stored"), sem("y3_free")
        var3_ready, std3_ready = sem("var3_ready"), sem("std3_ready")
        h1T_made, h1T_ready = sem("h1T_made"), sem("h1T_ready")
        att_made = sem("att_made")
        negmax_ready = sem("negmax_ready")
        probs_exp = sem("probs_exp")
        probs_ready = sem("probs_ready")
        probsT_made, probsT_ready = sem("probsT_made"), sem("probsT_ready")
        ca_made = sem("ca_made")
        var2_ready, std2_ready = sem("var2_ready"), sem("std2_ready")
        h2_ready = sem("h2_ready")
        h2T_made, h2T_ready = sem("h2T_made"), sem("h2T_ready")
        pq_made, pq_ready = sem("pq_made"), sem("pq_ready")
        keyscores_made, keyscores_ready = sem("keyscores_made"), sem("keyscores_ready")
        gate_logits, gate_exp = sem("gate_logits"), sem("gate_exp")
        idx_ready = sem("idx_ready")
        front_step = sem("front_step")
        tail_step = sem("tail_step")
        waits_passed = [sem("pool_waits_passed"), sem("dve_waits_passed")]

        def tiles(engine, body, last):
            body(0, 0, True)
            with engine.Fori(0, (TILES - 2) // 2) as i:
                body(2 * i + 1, 1, True)
                body(2 * i + 2, 0, True)
            body(TILES - 1, 1, False)
            last(TILES, 0)

        def late(t):
            return FIRST_LATE if isinstance(t, int) and t == 0 else 0

        def lagged(t, s, n):
            return (t, s, n - LAG) if n >= LAG else (t - 1, 1 - s, PICKS + n - LAG)

        with nc.Block() as block:
            @block.sync
            def _(sp):
                sp.sem_inc(y3_free, 1)

                def next_h1(t):
                    sp.wait_ge(h2_ready, t)
                    sp.dma_start(h1[:, :], h1_dram[t]).then_inc(h1_loaded, 16)

                def store_y3(t):
                    sp.wait_ge(y3_ready, t)
                    sp.dma_start(out[t - 1], y3[:, :]).then_inc(y3_stored, 16)
                    sp.wait_ge(y3_stored, 16 * t)
                    sp.sem_inc(y3_free, 1)

                next_h1(1)
                with sp.Fori(1, TILES - 1) as t:
                    next_h1(t + 1)
                    store_y3(t)
                store_y3(TILES - 1)
                sp.wait_ge(y3_ready, TILES)
                sp.dma_start(out[TILES - 1], y3[:, :]).then_inc(y3_stored, 16)
                sp.wait_ge(y3_stored, 16 * TILES)

            @block.gpsimd
            def _(pool):
                def gather(ring, landed, table, s, n):
                    pool.indirect_dma_start(out=ring[:, n % RING, :], out_offset=None, in_=table,
                                            in_offset=bass.IndirectOffsetOnAxis(ap=idx[:, s, n:n + 1], axis=0)
                                            ).then_inc(landed[n % RING], 16)

                def gather_u(t, s, n):
                    if isinstance(t, int) and t == 0 and n in (0, FIRST_HEADS * TOPK):
                        pool.wait_ge(idx_ready, 1 if n == 0 else 2)
                    elif n == 0:
                        pool.wait_ge(idx_ready, t + 2)
                    if not (isinstance(t, int) and PICKS * t + n < RING):
                        pool.wait_ge(dot_done, PICKS * t + n - RING + 1)
                        pool.sem_inc(waits_passed[0], 1)
                    gather(u_ring, u_landed, peer_u, s, n)

                def gather_v(t, s, n):
                    if not (isinstance(t, int) and PICKS * t + n < RING):
                        pool.wait_ge(v_used, PICKS * t + n - RING + 1)
                        pool.sem_inc(waits_passed[0], 1)
                    gather(v_ring, v_landed, peer_v, s, n)

                def body(t, s, front):
                    for n in range(PICKS):
                        gather_u(t, s, n)
                        if n >= LAG or not (isinstance(t, int) and t == 0):
                            gather_v(*lagged(t, s, n))

                def last(t, s):
                    for n in range(LAG):
                        gather_v(*lagged(t, s, n))

                tiles(pool, body, last)

            @block.tensor
            def _(pe):
                def combine(t, s, n):
                    pe.wait_ge(diag_ready, PICKS * t + n + 1)
                    pe.wait_ge(v_landed[n % RING], 16 * (PICKS // RING * t + n // RING + 1))
                    if n == 0 and not (isinstance(t, int) and t == 0):
                        pe.wait_ge(acc_copied, t)
                    for c in range(2):
                        last = pe.matmul(acc[:, c * 512:(c + 1) * 512], diag[:, n % RING, :],
                                         v_ring[:, n % RING, c * 512:(c + 1) * 512],
                                         start=(n == 0), stop=(n == PICKS - 1))
                    last.then_inc(v_used, 1)

                def to_T(source):
                    for k in range(KC):
                        last = pe.transpose(small[:, k * P:(k + 1) * P], source[:, k * P:(k + 1) * P], ident[:, :])
                    return last

                def front(f, s, n):
                    if n == 18:
                        pe.wait_ge(h1_loaded, 16 * (f + 1))
                        if not (isinstance(f, int) and f == 0):
                            pe.wait_ge(pq_ready, f)
                        to_T(h1).then_inc(h1T_made, 1)
                    if 22 <= n < 30:
                        q = n - 22
                        if q == 0:
                            pe.wait_ge(h1T_ready, f + 1)
                            if not (isinstance(f, int) and f == 0):
                                pe.wait_ge(keyscores_ready, f)
                        for k in range(2 * (q % 4), 2 * (q % 4) + 2):
                            c = q // 4
                            last = pe.matmul(wide[:, c * 512:(c + 1) * 512], hT[:, k, :],
                                             mem_scores_w[:, k, c * 512:(c + 1) * 512],
                                             start=(k == 0), stop=(k == KC - 1))
                        if q == 7:
                            last.then_inc(att_made, 1)
                    if n == 40:
                        pe.wait_ge(probs_ready, f + 1)
                        to_T(probs).then_inc(probsT_made, 1)
                    if 44 <= n < 52:
                        q = n - 44
                        if q == 0:
                            pe.wait_ge(probsT_ready, f + 1)
                        for k in range(2 * (q % 4), 2 * (q % 4) + 2):
                            c = q // 4
                            last = pe.matmul(wide[:, D + c * 512:D + (c + 1) * 512],
                                             probsT[:, k * P:(k + 1) * P],
                                             mem_values_w[:, k, c * 512:(c + 1) * 512],
                                             start=(k == 0), stop=(k == KC - 1))
                        if q == 7:
                            last.then_inc(ca_made, 1)
                    if n == 62:
                        pe.wait_ge(h2_ready, f + 1)
                        to_T(h2[:, s, :]).then_inc(h2T_made, 1)
                    if 66 <= n < 82:
                        q = n - 66
                        if q == 0:
                            pe.wait_ge(h2T_ready, f + 1)
                            pe.wait_ge(pwq_loaded, 16)
                        for k in range(4 * (q % 2), 4 * (q % 2) + 4):
                            h = q // 2
                            last = pe.matmul(small[:, h * P:(h + 1) * P], pwq[:, k, h * P:(h + 1) * P],
                                             hT[:, k, :], start=(k == 0), stop=(k == KC - 1))
                        if q == 15:
                            last.then_inc(pq_made, 1)
                    if 86 <= n < 90:
                        q = n - 86
                        if q == 0:
                            pe.wait_ge(pq_ready, f + 1)
                        for r in range(4 * q, 4 * q + 4):
                            half, h = r // PHEADS, r % PHEADS
                            last = pe.matmul(wide[:, r * NKEYS:(r + 1) * NKEYS],
                                             pqT[64 * half:64 * half + 64, h, :],
                                             keys[64 * half:64 * half + 64, :], start=True, stop=True)
                        if q == 3:
                            last.then_inc(keyscores_made, 1)

                pe.wait_ge(consts_loaded, 65)
                for n in range(PICKS):
                    front(0, 0, n)

                def body(t, s, next_front):
                    for n in range(PICKS):
                        if n >= LAG or not (isinstance(t, int) and t == 0):
                            combine(*lagged(t, s, n))
                        if next_front:
                            front(t + 1, 1 - s, n - late(t))

                def last(t, s):
                    for n in range(LAG):
                        combine(*lagged(t, s, n))

                tiles(pe, body, last)

            @block.scalar
            def _(act):
                def gelus(t, h):
                    act.wait_ge(dot_done, PICKS * t + TOPK * (h + 1))
                    act.activation(gelu_u[:, h % 2, :], act_u[:, h % 2, :], ACT.Gelu).then_inc(gelu_done, 1)

                def spread(t, s, n):
                    h, j = n // TOPK, n % TOPK
                    if j == 0:
                        act.wait_ge(w_ready, PHEADS * t + h + 1)
                    if not (isinstance(t, int) and PICKS * t + n < RING):
                        act.wait_ge(v_used, PICKS * t + n - RING + 1)
                    act.activation(diag[:, n % RING, :], ident[:, :], ACT.Copy,
                                   scale=w_v[:, h % 2, j:j + 1]).then_inc(diag_ready, 1)

                def front(f, s, n):
                    if n == 20:
                        act.wait_ge(h1T_made, f + 1)
                        act.activation(hT[:, :, :].rearrange("p k t -> p (k t)"), small[:, :],
                                       ACT.Copy).then_inc(h1T_ready, 1)
                    if n == 34:
                        act.wait_ge(negmax_ready, f + 1)
                        for h in range(HEADS_CA):
                            last = act.activation(probs[:, h * MEM:(h + 1) * MEM], wide[:, h * MEM:(h + 1) * MEM],
                                                  ACT.Exp, bias=negmax[:, h:h + 1], scale=MEM_SCALE,
                                                  accum_out=psums[:, h:h + 1])
                        last.then_inc(probs_exp, 1)
                    if n == 42:
                        act.wait_ge(probsT_made, f + 1)
                        act.activation(probsT, small[:, :], ACT.Copy).then_inc(probsT_ready, 1)
                    if n == 57:
                        act.wait_ge(var2_ready, f + 1)
                        act.activation(std[:, 0:1], moments[:, 0, 1:2], ACT.Sqrt,
                                       bias=eps[:, :]).then_inc(std2_ready, 1)
                    if n == 64:
                        act.wait_ge(h2T_made, f + 1)
                        act.activation(hT[:, :, :].rearrange("p k t -> p (k t)"), small[:, :],
                                       ACT.Copy).then_inc(h2T_ready, 1)
                    if n == 84:
                        act.wait_ge(pq_made, f + 1)
                        act.activation(pqT[:, :, :].rearrange("p h t -> p (h t)"), small[:, :],
                                       ACT.Copy).then_inc(pq_ready, 1)
                    if n == 91:
                        act.wait_ge(keyscores_made, f + 1)
                        for c in range(2):
                            last = act.activation(scores[:, c * D:(c + 1) * D], wide[:, c * D:(c + 1) * D], ACT.Copy)
                        last.then_inc(keyscores_ready, 1)
                    if n == 118:
                        if isinstance(f, int) and f == 0:
                            gate_exps(range(FIRST_HEADS), 1)
                        else:
                            gate_exps(range(PHEADS), f + 2)

                def gate_exps(hs, turn):
                    act.wait_ge(gate_logits, turn)
                    act.activation(gexp[:, hs[0]:hs[-1] + 1, :], gexp[:, hs[0]:hs[-1] + 1, :],
                                   ACT.Exp).then_inc(gate_exp, 1)

                act.wait_ge(consts_loaded, 65)
                for n in range(PICKS):
                    front(0, 0, n)

                def norm3(t):
                    act.wait_ge(var3_ready, t)
                    act.activation(std[:, 1:2], moments[:, 1, 1:2], ACT.Sqrt, bias=eps[:, :]).then_inc(std3_ready, 1)

                def body(t, s, next_front):
                    for n in range(PICKS):
                        if n % TOPK == 0 and n > 0:
                            gelus(t, n // TOPK - 1)
                        elif n == 0 and not (isinstance(t, int) and t == 0):
                            gelus(t - 1, PHEADS - 1)
                        if n >= LAG or not (isinstance(t, int) and t == 0):
                            spread(*lagged(t, s, n))
                        if n == LAG + 1 and not (isinstance(t, int) and t == 0):
                            norm3(t)
                        if isinstance(t, int) and t == 0 and n == FIRST_TOPK_AT[-4] + 1:
                            gate_exps(range(FIRST_HEADS, PHEADS), 2)
                        if next_front:
                            front(t + 1, 1 - s, n - late(t))

                def last(t, s):
                    gelus(t - 1, PHEADS - 1)
                    for n in range(LAG):
                        spread(*lagged(t, s, n))
                    norm3(t)

                tiles(act, body, last)

            @block.vector
            def _(dve):
                def dot(t, s, n):
                    dve.wait_ge(u_landed[n % RING], 16 * (PICKS // RING * t + n // RING + 1))
                    row = u_ring[:, n % RING, :]
                    dve.tensor_tensor_reduce(out=row, in0=row, in1=h2[:, s, :], scale=1.0, scalar=0.0,
                                             op0=ALU.mult, op1=ALU.add,
                                             accum_out=act_u[:, (n // TOPK) % 2, n % TOPK:n % TOPK + 1]
                                             ).then_inc(dot_done, 1)

                def weigh(t, s, h):
                    dve.wait_ge(gelu_done, PHEADS * t + h + 1)
                    if not (isinstance(t, int) and PHEADS * t + h < 2):
                        dve.wait_ge(diag_ready, PICKS * t + TOPK * (h - 1))
                    dve.tensor_tensor(w_v[:, h % 2, :], gelu_u[:, h % 2, :], gates[:, s, h * TOPK:(h + 1) * TOPK],
                                      ALU.mult).then_inc(w_ready, 1)

                def norm_stats(x, which, step, at):
                    for c in range(2):
                        last = dve.bn_stats(stats[:, which, c, :], x[:, c * 512:(c + 1) * 512])
                    last.then_inc(step, 1)
                    dve.wait_ge(step, at)
                    dve.sem_inc(waits_passed[1], 1)
                    return dve.bn_aggr(moments[:, which, :], stats[:, which, :, :].rearrange("p c s -> p (c s)"))

                def norm_apply(to, x, which, step, at):
                    dve.reciprocal(rstd[:, which:which + 1], std[:, which:which + 1]).then_inc(step, 1)
                    dve.wait_ge(step, at)
                    dve.tensor_scalar(x, x, moments[:, which, 0:1], rstd[:, which:which + 1],
                                      ALU.subtract, ALU.mult).then_inc(step, 1)
                    dve.wait_ge(step, at + 1)
                    dve.tensor_tensor(x, x, ln[:, 2 * which, :], ALU.mult).then_inc(step, 1)
                    dve.wait_ge(step, at + 2)
                    return dve.tensor_tensor(to, x, ln[:, 2 * which + 1, :], ALU.add)

                def norm3_first(t):
                    at = TAIL_STEPS * (t - 1)
                    dve.wait_ge(v_used, PICKS * t)
                    dve.wait_ge(y3_free, t)
                    return at

                def norm3_a(t, s):
                    at = norm3_first(t)
                    dve.scalar_tensor_tensor(y3[:, :], h2[:, s, :], ALPHA, acc[:, :], ALU.mult,
                                             ALU.add).then_inc(acc_copied, 1)
                    dve.wait_ge(acc_copied, t)
                    norm_stats(y3[:, :], 1, tail_step, at + 1).then_inc(var3_ready, 1)

                def norm3_b(t):
                    at = TAIL_STEPS * (t - 1)
                    dve.wait_ge(std3_ready, t)
                    norm_apply(y3[:, :], y3[:, :], 1, tail_step, at + 2).then_inc(y3_ready, 1)

                def link_from(at):
                    def link(ins, k):
                        ins.then_inc(front_step, 1)
                        dve.wait_ge(front_step, at + k)
                        dve.sem_inc(waits_passed[1], 1)
                    return link

                def front(f, s, n):
                    at = FRONT_STEPS * f + (0 if isinstance(f, int) and f == 0 else FIRST_STEPS)
                    link = link_from(at)
                    if n == 32:
                        dve.wait_ge(att_made, f + 1)
                        link(dve.tensor_reduce(rowmax[:, :], wide[:, 0:D].rearrange("p (h m) -> p h m", m=MEM),
                                               AX, ALU.max), 1)
                        dve.tensor_scalar(negmax[:, :], rowmax[:, :], -MEM_SCALE, None,
                                          ALU.mult).then_inc(negmax_ready, 1)
                    if n == 37:
                        dve.wait_ge(probs_exp, f + 1)
                        link(dve.reciprocal(pinv[:, :], psums[:, :]), 2)
                        p4 = probs.rearrange("p (h m) -> p h m", m=MEM)
                        dve.tensor_tensor(p4, p4, pinv[:, :].unsqueeze(2).to_broadcast([P, HEADS_CA, MEM]),
                                          ALU.mult).then_inc(probs_ready, 1)
                    if n == 54:
                        dve.wait_ge(ca_made, f + 1)
                        link(dve.scalar_tensor_tensor(pre2, h1[:, :], ALPHA, wide[:, D:2 * D], ALU.mult,
                                                      ALU.add), 3)
                        norm_stats(pre2, 0, front_step, at + 4).then_inc(var2_ready, 1)
                    if n == 59:
                        dve.wait_ge(std2_ready, f + 1)
                        norm_apply(h2[:, s, :], pre2, 0, front_step, at + 5).then_inc(h2_ready, 1)
                    if n in TOPK_AT and not (isinstance(f, int) and f == 0):
                        top_picks(f, s, link, TOPK_AT.index(n), range(PHEADS), f + 2)

                def top_picks(f, s, link, piece, hs, turn):
                    G, h0, h1 = len(hs), hs[0], hs[-1] + 1
                    picks = slice(h0 * TOPK, h1 * TOPK)
                    rows = [half * PHEADS + h for half in range(2) for h in hs]
                    apart = G < PHEADS and h0 == 0
                    size = G * TOPK * TOPK
                    sums = scores_cut[:, 0:size] if apart else scores[:, h0 * MEM:h0 * MEM + size]
                    sums_cut = scores_cut[:, D:D + size] if apart else scores_cut[:, h0 * MEM:h0 * MEM + size]
                    cand = [sums[:, g * TOPK * TOPK:(g + 1) * TOPK * TOPK] for g in range(G)]
                    cut = [sums_cut[:, g * TOPK * TOPK:(g + 1) * TOPK * TOPK] for g in range(G)]
                    pos = (1 if apart else 0)
                    raw = [slice(r * NKEYS, (r + 1) * NKEYS) for r in rows]
                    if piece == 0:
                        dve.wait_ge(keyscores_ready, f + 1)
                        dve.wait_ge(h2_ready, f + 1)
                        dve.sem_inc(waits_passed[1], 1)
                        for r, w in zip(rows, raw):
                            last = dve.max(vals[:, r, 0:8], scores[:, w])
                        link(last, 8)
                    if piece == 1:
                        for r, w in zip(rows, raw):
                            dve.max_index(vidx[:, r, 0:8], vals[:, r, 0:8], scores[:, w])
                    if piece == 2:
                        for r, w in zip(rows, raw):
                            last = dve.match_replace(scores_cut[:, w], vals[:, r, 0:8], scores[:, w], LEAST)
                        link(last, 9)
                    if piece == 3:
                        for r, w in zip(rows, raw):
                            last = dve.max(vals[:, r, 8:16], scores_cut[:, w])
                        link(last, 10)
                    if piece == 4:
                        for r, w in zip(rows, raw):
                            last = dve.max_index(vidx[:, r, 8:16], vals[:, r, 8:16], scores_cut[:, w])
                        if apart:
                            link(last, 11)
                        v4 = vals[:, :, :].rearrange("p (c h) k -> p c h k", c=2)
                        link(dve.tensor_tensor(sums.rearrange("p (h i j) -> p h i j", i=TOPK, j=TOPK),
                                               v4[:, 0, hs[0]:h1, :].unsqueeze(3).to_broadcast([P, G, TOPK, TOPK]),
                                               v4[:, 1, hs[0]:h1, :].unsqueeze(2).to_broadcast([P, G, TOPK, TOPK]),
                                               ALU.add), 11 + pos)
                    if piece == 5:
                        for g, h in enumerate(hs):
                            last = dve.max(best[:, h, 0:8], cand[g])
                        link(last, 12 + pos)
                    if piece == 6:
                        for g, h in enumerate(hs):
                            dve.max_index(bidx[:, h, 0:8], best[:, h, 0:8], cand[g])
                    if piece == 7:
                        for g, h in enumerate(hs):
                            last = dve.match_replace(cut[g], best[:, h, 0:8], cand[g], LEAST)
                        link(last, 13 + pos)
                    if piece == 8:
                        for g, h in enumerate(hs):
                            last = dve.max(best[:, h, 8:16], cut[g])
                        link(last, 14 + pos)
                    if piece == 9:
                        for g, h in enumerate(hs):
                            last = dve.max_index(bidx[:, h, 8:16], best[:, h, 8:16], cut[g])
                        link(last, 15 + pos)
                        flat = bidx[:, h0:h1, :].rearrange("p h k -> p (h k)")
                        dve.tensor_scalar(bhalf[:, 0, picks], flat, 4, None, ALU.logical_shift_right)
                        dve.tensor_scalar(bhalf[:, 1, picks], flat, 15, None, ALU.bitwise_and)
                        dve.tensor_copy(vidx_f[:, :, :].rearrange("p (c h) k -> p c h k", c=2)[:, :, h0:h1, :],
                                        vidx[:, :, :].rearrange("p (c h) k -> p c h k", c=2)[:, :, h0:h1, :])
                        dve.tensor_tensor(gexp[:, h0:h1, :], best[:, h0:h1, :],
                                          best[:, h0:h1, 0:1].to_broadcast([P, G, TOPK]),
                                          ALU.subtract).then_inc(gate_logits, 1)
                        dve.wait_ge(gate_logits, turn)
                        link(dve.tensor_copy(bhalf_f[:, :, picks], bhalf[:, :, picks]), 16 + pos)
                    for half, where in enumerate((sums_cut, sums)):
                        if piece == 10 + half:
                            n = G * TOPK
                            w4 = where.rearrange("p (h k j) -> p h k j", k=TOPK, j=TOPK)
                            w3 = where.rearrange("p (a j) -> p a j", j=TOPK)
                            link(dve.tensor_tensor(w3, bhalf_f[:, half, picks].unsqueeze(2).to_broadcast([P, n, TOPK]),
                                                   iota16[:, :].unsqueeze(1).to_broadcast([P, n, TOPK]),
                                                   ALU.is_equal), 17 + 3 * half + pos)
                            names = vidx_f[:, half * PHEADS + h0:half * PHEADS + h1, :]
                            link(dve.tensor_tensor(w4, w4, names.unsqueeze(2).to_broadcast([P, G, TOPK, TOPK]),
                                                   ALU.mult), 18 + 3 * half + pos)
                            link(dve.tensor_reduce(ihalf[:, half, picks], w3, AX, ALU.add), 19 + 3 * half + pos)
                    if piece == 12:
                        dve.scalar_tensor_tensor(idx[:, s, picks], ihalf[:, 0, picks], float(NKEYS),
                                                 ihalf[:, 1, picks], ALU.mult, ALU.add).then_inc(idx_ready, 1)
                    if piece == 13:
                        dve.wait_ge(gate_exp, turn)
                        link(dve.tensor_reduce(gsum[:, h0:h1], gexp[:, h0:h1, :], AX, ALU.add), 23 + pos)
                        link(dve.reciprocal(ginv[:, h0:h1], gsum[:, h0:h1]), 24 + pos)
                        link(dve.tensor_tensor(gates[:, s, picks].rearrange("p (h k) -> p h k", k=TOPK),
                                               gexp[:, h0:h1, :],
                                               ginv[:, h0:h1].unsqueeze(2).to_broadcast([P, G, TOPK]),
                                               ALU.mult), 25 + pos)

                dve.memset(eps[:, :], LN_EPS).then_inc(consts_loaded, 1)
                dve.wait_ge(consts_loaded, 65)
                for n in range(TOPK_AT[0]):
                    front(0, 0, n)
                for piece in range(len(TOPK_AT)):
                    top_picks(0, 0, link_from(0), piece, range(FIRST_HEADS), 1)

                def body(t, s, next_front):
                    for n in range(PICKS):
                        dot(t, s, n)
                        if isinstance(t, int) and t == 0 and n in FIRST_TOPK_AT:
                            top_picks(0, 0, link_from(FIRST_STEPS), FIRST_TOPK_AT.index(n), range(FIRST_HEADS, PHEADS), 2)
                        if n % TOPK == 2 and n > TOPK:
                            weigh(t, s, n // TOPK - 1)
                        elif n == 2 and not (isinstance(t, int) and t == 0):
                            weigh(t - 1, 1 - s, PHEADS - 1)
                        if n == LAG and not (isinstance(t, int) and t == 0):
                            norm3_a(t, 1 - s)
                        if n == LAG + 4 and not (isinstance(t, int) and t == 0):
                            norm3_b(t)
                        if next_front:
                            front(t + 1, 1 - s, n - late(t))

                def last(t, s):
                    weigh(t - 1, 1 - s, PHEADS - 1)
                    norm3_a(t, 1 - s)
                    norm3_b(t)

                tiles(dve, body, last)


def program(nc, a, out):
    scanT = nc.dram_tensor("scanT_dram", (2 * GLA_BLOCKS + XBC_BLOCKS + GLA_BLOCKS, P, SEQ), F32).ap()
    nat = nc.dram_tensor("nat_dram", (3, TILES, P, D), F32).ap()
    h1 = nc.dram_tensor("h1_dram", (TILES, P, D), F32).ap()
    with ExitStack() as ctx:
        sb, psum, sem = allocators(nc, ctx)
        scalars = sb("scalars", [P, TILES, KINDS, HEADS_SSD], F32)
        project_inputs(nc, a, scanT, nat, scalars)
        mix_tokens(nc, a, scanT, nat, scalars, h1)
    with ExitStack() as ctx:
        sb, psum, sem = allocators(nc, ctx)
        mem_scores_w = sb("mem_scores_w", [P, KC, D], F32)
        mem_values_w = sb("mem_values_w", [P, KC, D], F32)
        kept = retrieval_constants(sb, sem)
        build_memory_tables(nc, a, h1, mem_scores_w, mem_values_w, kept)
        attend_and_retrieve(nc, h1, a["u"], a["v"], out, mem_scores_w, mem_values_w, kept)


def kernel(**inputs):
    import numpy as np
    import concourse.bacc as _bacc
    from concourse import mybir as _mybir
    from concourse.bass_utils import run_bass_kernel_spmd as _run

    x = {k: np.asarray(v) for k, v in inputs.items()}

    def chunks(w):
        return w.reshape(-1, P, w.shape[-1]).transpose(1, 0, 2)

    def rows(*v):
        return np.broadcast_to(np.stack(v)[None], (P, len(v), v[0].shape[-1]))

    def columns(v):
        return v.reshape(-1, P).T

    w_in = x["w_in"][0]
    q0, k0, v0, r0, g0, z0, c0, t0 = 0, 512, 1024, 2048, 3072, 3088, 4112, 5392
    w_tr = np.concatenate([w_in[:, q0:v0], w_in[:, c0:t0]], 1)
    w_nat = np.concatenate([w_in[:, v0:g0], w_in[:, z0:c0]], 1)
    u = np.arange(P)
    masks = [((u[None] >> lv) % 2 == 1) & ((u[:, None] >> lv) == (u[None] >> lv) - 1) for lv in range(LEVELS)]
    masks.append(u[:, None] == u[None])
    import ml_dtypes
    given = {
        "x": x["x"].reshape(TILES, P, D),
        "xT": chunks(x["x"][0].T),
        "w_low": np.stack([chunks(w_in[:, g0:g0 + RANK]), chunks(w_in[:, t0:t0 + RANK])], 2),
        "w_tr": np.stack([chunks(w_tr[:, i:i + P]) for i in range(0, w_tr.shape[1], P)]),
        "w_nat": np.stack([chunks(w_nat[:, i:i + 512]) for i in range(0, w_nat.shape[1], 512)]),
        "wg2": x["gla_wg2"][0],
        "small_cols": np.concatenate([columns(x["gla_bg"][0]),
                                      x["ssd_conv_w"][0].T.reshape(XBC_BLOCKS, P, CONV).transpose(1, 0, 2)
                                      .reshape(P, -1), columns(x["ssd_conv_b"][0])], 1),
        "small_rows": rows(x["ssd_dt_bias"][0], x["ssd_a_log"][0]),
        "tri": (u[:, None] <= u[None]).astype(np.float32),
        "ident16": np.eye(P, dtype=ml_dtypes.bfloat16),
        "future16": np.where(u[:, None] > u[None], -1e30, 0.0).astype(ml_dtypes.bfloat16),
        "level_mask": np.stack(masks, 1).astype(ml_dtypes.bfloat16),
        "gainT": columns(np.concatenate([np.tile(x["gla_norm_g"][0], GLA_BLOCKS), x["ssd_norm_g"][0]])),
        "d_row": np.broadcast_to(x["ssd_d"][0], (P, HEADS_SSD)),
        "ln1": rows(x["ln1_g"][0], x["ln1_b"][0]),
        "w_out": chunks(x["w_out"][0]),
        "memT": chunks(x["mem"][0].T),
        "wk": chunks(x["ca_wk"][0]), "wqT": chunks(x["ca_wq"][0].T), "wv": chunks(x["ca_wv"][0]),
        "wo": chunks(x["ca_wo"][0]), "peer_wq": chunks(x["peer_wq"][0]),
        "keysT": x["peer_keys"][0].transpose(0, 2, 1).reshape(P, NKEYS),
        "u": x["peer_u"][0], "v": x["peer_v"][0],
        "ln": rows(x["ln2_g"][0], x["ln2_b"][0], x["ln3_g"][0], x["ln3_b"][0]),
        "ident": np.eye(P, dtype=np.float32),
        "iota": np.broadcast_to(np.arange(TOPK, dtype=np.float32), (P, TOPK)),
    }
    nc = _bacc.Bacc("TRN2", target_bir_lowering=False, num_devices=1)
    arrays, args = {}, {}
    for name, v in given.items():
        v = np.ascontiguousarray(v)
        arrays[f"in_{name}_dram"] = v
        args[name] = nc.dram_tensor(f"in_{name}_dram", v.shape, _mybir.dt.from_np(v.dtype), kind="ExternalInput").ap()
    out = nc.dram_tensor("out_0_dram", (TILES, P, D), F32, kind="ExternalOutput").ap()
    program(nc, args, out)
    r = _run(nc, [arrays], core_ids=[0])
    return r.results[0]["out_0_dram"].reshape(1, SEQ, D)
```
